# Optimizing a Trainium2 kernel written in Bass

```python
import jax, jax.numpy as jnp
from jax import lax
import numpy as np

D_MODEL = 1024
BATCH = 1
SEQ = 512
DEPTH = 2

MIX_WIDTH = D_MODEL
CONV_WIDTH = MIX_WIDTH // 2
CONV_GROUPS = 8
CONV_K = 3
RET_HEADS = 4
RET_WIDTH = MIX_WIDTH - CONV_WIDTH
RET_HEAD_DIM = RET_WIDTH // RET_HEADS
CHUNK = 128
D_FF = 4 * D_MODEL
ROPE_BASE = 10000.0
EPS = 1e-6
N_MOD = 6
IN_SIZES = (CONV_WIDTH, CONV_WIDTH, CONV_WIDTH, RET_WIDTH, RET_WIDTH, RET_WIDTH, RET_WIDTH)
IN_COLS = sum(IN_SIZES)
IN_SPLITS = [int(s) for s in np.cumsum(IN_SIZES)[:-1]]

kernel_name = "hybrid_shortconv_retention_adaln_trunk"

def rms_norm(x, g):
    xf = x.astype(jnp.float32)
    y = xf * lax.rsqrt(jnp.mean(xf * xf, axis=-1, keepdims=True) + EPS)
    return (y * g.astype(jnp.float32)).astype(x.dtype)

def rope_tables(t, d):
    inv_freq = ROPE_BASE ** (-jnp.arange(0, d, 2, dtype=jnp.float32) / d)
    ang = jnp.arange(t, dtype=jnp.float32)[:, None] * inv_freq[None, :]
    return jnp.cos(ang), jnp.sin(ang)

def apply_rope(u, cos, sin):
    half = u.shape[-1] // 2
    u1, u2 = u[..., :half], u[..., half:]
    cs, sn = cos[None, :, None, :], sin[None, :, None, :]
    return jnp.concatenate([u1 * cs - u2 * sn, u1 * sn + u2 * cs], axis=-1)

def short_conv(u, w):
    return lax.conv_general_dilated(
        u, w[:, None, :].astype(u.dtype), window_strides=(1,),
        padding=[(CONV_K - 1, 0)], dimension_numbers=('NWC', 'WIO', 'NWC'),
        feature_group_count=u.shape[-1])

def retention_chunkwise(q, k, v):
    b, t, h, d = q.shape
    n = t // CHUNK
    log_g = jnp.log1p(-jnp.exp2(-5.0 - jnp.arange(h, dtype=jnp.float32)))
    idx = jnp.arange(CHUNK, dtype=jnp.float32)
    diff = idx[:, None] - idx[None, :]
    causal = diff >= 0
    inner_decay = jnp.where(causal[None],
                            jnp.exp(log_g[:, None, None] * jnp.where(causal, diff, 0.0)[None]),
                            0.0)
    xi = jnp.exp(log_g[:, None] * (idx + 1.0)[None])
    zeta = jnp.exp(log_g[:, None] * (CHUNK - 1.0 - idx)[None])
    chunk_decay = jnp.exp(log_g * CHUNK)

    qc = q.reshape(b, n, CHUNK, h, d)
    kc = k.reshape(b, n, CHUNK, h, d)
    vc = v.reshape(b, n, CHUNK, h, d)
    scores = jnp.einsum('bnihd,bnjhd->bnhij', qc, kc) * inner_decay[None, None]
    inner = jnp.einsum('bnhij,bnjhe->bnihe', scores, vc)
    kv = jnp.einsum('bnjhd,bnjhe,hj->nbhde', kc, vc, zeta)

    def step(state, kv_n):
        return state * chunk_decay[None, :, None, None] + kv_n, state

    _, states = lax.scan(step, jnp.zeros((b, h, d, d), jnp.float32), kv)
    cross = jnp.einsum('bnihd,nbhde,hi->bnihe', qc, states, xi)
    return (inner + cross).reshape(b, t, h, d)

def setup_inputs(seed: int = 0) -> dict:
    key = jax.random.key(seed)
    ks = jax.random.split(key, 14)
    f32 = jnp.float32
    x = jax.random.normal(ks[0], (BATCH, SEQ, D_MODEL), f32)
    c = jax.random.normal(ks[1], (BATCH, D_MODEL), f32)
    norm1_g = 1.0 + 0.05 * jax.random.normal(ks[2], (DEPTH, D_MODEL), f32)
    w_in = jax.random.normal(ks[3], (DEPTH, D_MODEL, IN_COLS), f32) * D_MODEL ** -0.5
    conv_w = jax.random.normal(ks[4], (DEPTH, CONV_K, CONV_WIDTH), f32) * CONV_K ** -0.5
    ret_norm_g = 1.0 + 0.05 * jax.random.normal(ks[5], (DEPTH, RET_WIDTH), f32)
    w_out = jax.random.normal(ks[6], (DEPTH, MIX_WIDTH, D_MODEL), f32) * MIX_WIDTH ** -0.5
    norm2_g = 1.0 + 0.05 * jax.random.normal(ks[7], (DEPTH, D_MODEL), f32)
    w_up = jax.random.normal(ks[8], (DEPTH, D_MODEL, D_FF), f32) * D_MODEL ** -0.5
    w_down = jax.random.normal(ks[9], (DEPTH, D_FF, D_MODEL), f32) * D_FF ** -0.5
    w_ada = jax.random.normal(ks[10], (DEPTH, D_MODEL, N_MOD * D_MODEL), f32) * (0.5 * D_MODEL ** -0.5)
    b_ada = 0.02 * jax.random.normal(ks[11], (DEPTH, N_MOD * D_MODEL), f32)
    final_g = 1.0 + 0.05 * jax.random.normal(ks[12], (D_MODEL,), f32)
    return {"x": x, "c": c, "norm1_g": norm1_g, "w_in": w_in, "conv_w": conv_w,
            "ret_norm_g": ret_norm_g, "w_out": w_out, "norm2_g": norm2_g,
            "w_up": w_up, "w_down": w_down, "w_ada": w_ada, "b_ada": b_ada,
            "final_g": final_g}

def reference(x, c, norm1_g, w_in, conv_w, ret_norm_g, w_out, norm2_g,
              w_up, w_down, w_ada, b_ada, final_g):
    b, t, _ = x.shape
    cos, sin = rope_tables(t, RET_HEAD_DIM)
    c_act = jax.nn.silu(c)
    for l in range(DEPTH):
        mod = (c_act @ w_ada[l] + b_ada[l])[:, None, :]
        sh1, sc1, g1, sh2, sc2, g2 = jnp.split(mod, N_MOD, axis=-1)

        h = rms_norm(x, norm1_g[l]) * (1.0 + sc1) + sh1
        proj = h @ w_in[l]
        cb, cc, cu, q, k, v, gr = jnp.split(proj, IN_SPLITS, axis=-1)

        y_conv = cb * short_conv(cc * cu, conv_w[l])

        qh = apply_rope(q.astype(jnp.float32).reshape(b, t, RET_HEADS, RET_HEAD_DIM), cos, sin)
        kh = apply_rope(k.astype(jnp.float32).reshape(b, t, RET_HEADS, RET_HEAD_DIM), cos, sin)
        kh = kh * (RET_HEAD_DIM ** -0.5)
        vh = v.astype(jnp.float32).reshape(b, t, RET_HEADS, RET_HEAD_DIM)
        o = retention_chunkwise(qh, kh, vh)
        mu = jnp.mean(o, axis=-1, keepdims=True)
        var = jnp.mean(jnp.square(o - mu), axis=-1, keepdims=True)
        o = ((o - mu) * lax.rsqrt(var + EPS)).reshape(b, t, RET_WIDTH)
        o = (o * ret_norm_g[l].astype(jnp.float32)).astype(x.dtype)
        y_ret = jax.nn.silu(gr) * o

        mix = jnp.concatenate([y_conv, y_ret], axis=-1) @ w_out[l]
        x = x + g1 * mix

        h2 = rms_norm(x, norm2_g[l]) * (1.0 + sc2) + sh2
        x = x + g2 * (jnp.square(jax.nn.relu(h2 @ w_up[l])) @ w_down[l])

    return rms_norm(x, final_g)


_drawn_inputs = setup_inputs


def setup_inputs(seed=0):
    import zlib

    import numpy as np

    out = dict(_drawn_inputs(seed))
    spreads = {}
    factors = {'ret_norm_g': 5.365}
    for name, (base, spread) in spreads.items():
        noise = np.random.default_rng([zlib.crc32(name.encode()), seed]).standard_normal(out[name].shape)
        drawn = base * np.exp(spread * noise) if base else spread * noise
        out[name] = __import__('jax').numpy.asarray(drawn.astype(out[name].dtype))
    for name, factor in factors.items():
        out[name] = (out[name] * factor).astype(out[name].dtype)
    return out
```

```python
from contextlib import ExitStack

import concourse.bass as bass
from concourse import mybir

P = 128
D = 1024
T = 512
DEPTH = 2
KT = D // P
HEADS = 4
EPS = 1e-6
SLOTS = 4
UNITS = 100
STEPS = UNITS // SLOTS
MODS = 6 * KT
FIRST_MODS = 2 * KT
HALF_TILES = 16

U_V, U_QK, U_HEAD, U_OUT = 0, 4, 12, 28
U_UP = (36, 68)
U_DOWN = (52, 84)
EA_V, EA_QK, EA_HEAD, EA_UP = 0, 4, 12, (20, 36)
EA = 52
ED_HEAD, ED_OUT, ED_DOWN = 0, 8, (16, 24)
ED = 32
XS_H, XS_Y, XS_H2, XS_U = 0, 8, 16, (24, 40)
XS = 56
C_G1, C_G2, C_CONV, C_RET = 0, 8, 16, 28
PARAMS = 32
M_SH1, M_SC1, M_GATE1, M_SH2, M_SC2, M_GATE2 = range(0, MODS, KT)

F32 = mybir.dt.float32
F32R = mybir.dt.float32r
ALU = mybir.AluOpType
ACT = mybir.ActivationFunctionType
AX_X = mybir.AxisListType.X


def trunk(nc, xT, c_rows, weights, ada, params, bias, final_g, tables, outT):
    with ExitStack() as ctx:
        def sb(name, shape, dt=F32):
            return ctx.enter_context(nc.sbuf_tensor(name, shape, dt))

        def sem(name):
            return ctx.enter_context(nc.semaphore(name))

        arena_at = -(-nc.sbuf_base // 32) * 32
        arena = sb("arena", [P, 16, D])
        over = [arena_at]

        def view(name, shape, dt=F32):
            size = 4
            for n in shape[1:]:
                size *= n
            t = nc.alloc_sbuf_tensor_at(name, shape, dt, offset=over[0])
            over[0] += size
            assert over[0] <= arena_at + 16 * D * 4
            return t

        u_hi = view("u_hi", [P, HALF_TILES, T], F32R)
        u_lo = view("u_lo", [P, HALF_TILES, T], F32R)
        over[0] = arena_at
        y_hi = view("y_hi", [P, KT, T], F32R)
        qk_at = over[0]
        qkT = view("qkT", [P, 2 * HEADS, T])
        v_T = view("v_T", [P, HEADS, T])
        v_tok = view("v_tok", [P, HEADS, T])
        k_cur = view("k_cur", [P, T])
        v_cur = view("v_cur", [P, T])
        s_T = view("s_T", [P, 1280])
        gr = view("gr", [P, T])
        egr = view("egr", [P, T])
        over[0] = qk_at
        y_lo = view("y_lo", [P, KT, T], F32R)

        x = sb("x", [P, KT, T])
        h_hi = sb("h_hi", [P, KT, T], F32R)
        h_lo = sb("h_lo", [P, KT, T], F32R)
        w_raw = sb("w_raw", [P, SLOTS, D])
        w_hi = sb("w_hi", [P, SLOTS, D], F32R)
        w_lo = sb("w_lo", [P, SLOTS, D], F32R)
        ada_raw = sb("ada_raw", [P, 2, D])
        tab = sb("tab", [P, tables.shape[1]])
        decay = tab[:, 0:HEADS * T].rearrange("p (h t) -> p h t", h=HEADS)
        cos = tab[:, HEADS * T:HEADS * T + T]
        sin = tab[:, HEADS * T + T:HEADS * T + 2 * T]
        ident = tab[:, HEADS * T + 2 * T:HEADS * T + 2 * T + P]
        c_act = sb("c_act", [P, D])
        par = sb("par", [P, DEPTH * PARAMS])
        bia = sb("bia", [P, DEPTH * MODS])
        fin_g = sb("fin_g", [P, KT])
        mod = sb("mod", [P, MODS])
        ada_sum = sb("ada_sum", [P, 2])
        gm = sb("gm", [P, 2, KT])
        eps = sb("eps", [P, 1])
        vsum = sb("vsum", [P, HEADS])
        mean_d = sb("mean_d", [P, P])
        mean_e = sb("mean_e", [P, P])
        buf_a = sb("buf_a", [P, 2, T])
        buf_b = sb("buf_b", [P, 2, T])
        ssum = sb("ssum", [P, T])
        std = sb("std", [P, T])
        rinv = sb("rinv", [P, T])
        z = sb("z", [P, T + 2])
        conv = sb("conv", [P, T])
        cc = ssum

        ps = ctx.enter_context(nc.psum_tensor("ps", [P, 8, T], F32))
        S_BANK = (4, 5, 6, 6)
        S_COL = (0, 0, 0, 256)
        S_AT = (0, 512, 896, 1152)
        STAT, O = 4, 7

        c_in, par_in, tab_in = sem("c_in"), sem("par_in"), sem("tab_in")
        x_in = sem("x_in")
        ada0_in = [sem(f"ada0_in{i}") for i in range(4)]
        w_in = [sem(f"w_in{i}") for i in range(SLOTS)]
        ada_in = [sem(f"ada_in{i}") for i in range(2)]
        consts = sem("consts")
        c_exp, c_step = sem("c_exp"), sem("c_step")
        w_hi_done = sem("w_hi_done")
        w_lo_done = sem("w_lo_done")
        pe_unit = sem("pe_unit")
        ada_done = sem("ada_done")
        ada0_done = sem("ada0_done")
        mod_added = sem("mod_added")
        evac_act = sem("evac_act")
        evac_dve = sem("evac_dve")
        xs_hi, xs_lo = sem("xs_hi"), sem("xs_lo")
        sq_ready = sem("sq_ready")
        ssum_added = sem("ssum_added")
        ssum_clear = sem("ssum_clear")
        stat_ps, norm_std, norm_r, gm_ready = sem("stat_ps"), sem("norm_std"), sem("norm_r"), sem("gm_ready")
        xr_ready, hf_ready = sem("xr_ready"), sem("hf_ready")
        rope_step = sem("rope_step")
        rope_done = sem("rope_done")
        v_turned, v_summed = sem("v_turned"), sem("v_summed")
        v_centered = sem("v_centered")
        cur_ready, s_ps, s_ready = sem("cur_ready"), sem("s_ps"), sem("s_ready")
        o_ps, o_read, std_ready = sem("o_ps"), sem("o_read"), sem("std_ready")
        osq_ready, var_ps = sem("osq_ready"), sem("var_ps")
        conv_step = sem("conv_step")
        gate_step = sem("gate_step")
        rsq_ready = sem("rsq_ready")
        out_ready, out_done = sem("out_ready"), sem("out_done")

        block = ctx.enter_context(nc.Block())

        def below(value, limit, size=1):
            return nc.s_assert_within(value, 0, limit - size,
                                      skip_runtime_bounds_check_because="under If(l < DEPTH - 1)")

        @block.sync
        def _(sp):
            def load_weights(l, step, ahead):
                for j in range(SLOTS):
                    load_weight(l, step, ahead, j)

            def load_weight(l, step, ahead, j):
                u = l * UNITS + step * SLOTS + (ahead * SLOTS + j)
                if ahead:
                    sp.wait_ge(w_lo_done, u + 1)
                sp.dma_start(w_raw[:, j, :], weights[bass.ds(below(u, DEPTH * UNITS), 1), :, :].rearrange("a p n -> p (a n)")
                             ).then_inc(w_in[j], 16)

            def load_ada(b, j):
                sp.wait_ge(ada_done, b + 1)
                sp.dma_start(ada_raw[:, j % 2, :],
                             ada[bass.ds(below(b + FIRST_MODS, DEPTH * MODS), 1), :, :].rearrange("a p n -> p (a n)")
                             ).then_inc(ada_in[j % 2], 16)

            def load_step(l, step, adas, b):
                for j in range(SLOTS):
                    load_weight(l, step, 1, j)
                    if j < adas:
                        load_ada(b + j, j)

            sp.dma_start(c_act[:], c_rows).then_inc(c_in, 16)
            sp.dma_start(arena[:, 0:4, :], ada[0:4, :, :].rearrange("a p n -> p a n")).then_inc(ada0_in[0], 16)
            sp.dma_start(par[:], params).then_inc(par_in, 16)
            sp.dma_start(bia[:], bias).then_inc(par_in, 16)
            sp.dma_start(fin_g[:], final_g).then_inc(par_in, 16)
            sp.dma_start(x[:], xT.rearrange("k p t -> p k t")).then_inc(x_in, 16)
            for i in range(1, 4):
                sp.dma_start(arena[:, 4 * i:4 * i + 4, :], ada[4 * i:4 * i + 4, :, :].rearrange("a p n -> p a n")
                             ).then_inc(ada0_in[i], 16)
            for j in range(SLOTS):
                sp.dma_start(w_raw[:, j, :], weights[j, :, :]).then_inc(w_in[j], 16)
            sp.dma_start(tab[:], tables).then_inc(tab_in, 16)

            with sp.Fori(0, DEPTH) as l:
                b0 = l * MODS
                load_step(l, 0, 0, 0)
                with sp.Fori(0, 6) as i:
                    load_step(l, i + 1, 4, b0 + i * 4)
                with sp.Fori(0, 2) as i:
                    load_step(l, i + 7, 0, 0)
                with sp.Fori(0, 4) as i:
                    load_step(l, i + 9, 2, b0 + i * 2 + 24)
                with sp.Fori(0, 8) as i:
                    load_weight(l, i + 13, 1, 0)
                    load_weight(l, i + 13, 1, 1)
                    with sp.If(l < DEPTH - 1):
                        load_ada(b0 + i * 2 + 32, 0)
                        load_ada(b0 + i * 2 + 33, 1)
                    load_weight(l, i + 13, 1, 2)
                    load_weight(l, i + 13, 1, 3)
                with sp.Fori(0, 3) as i:
                    load_step(l, i + 21, 0, 0)
                with sp.If(l < DEPTH - 1):
                    load_step(l, 24, 0, 0)

            for k in range(KT):
                sp.wait_ge(out_ready, k + 1)
                sp.dma_start(outT[k, :, :], x[:, k, :]).then_inc(out_done, 16)
            sp.wait_ge(out_done, 16 * KT)

        @block.tensor
        def _(pe):
            def three(bank, j, k, hi, lo, first, last):
                wh, wl = w_hi[:, j, k * P:(k + 1) * P], w_lo[:, j, k * P:(k + 1) * P]
                nc.tensor.matmul(ps[:, bank, :], wh, hi, start=first, stop=False)
                nc.tensor.matmul(ps[:, bank, :], wh, lo, start=False, stop=False)
                return nc.tensor.matmul(ps[:, bank, :], wl, hi, start=False, stop=last)

            def unit(u, j, bank, hi, lo, k0=0, first=True, last=True):
                pe.wait_ge(w_lo_done, u + (SLOTS + 1))
                for k in range(KT):
                    mm = three(bank, j, k, hi[:, k0 + k, :], lo[:, k0 + k, :], first and k == 0, last and k == KT - 1)
                mm.then_inc(pe_unit, 1)

            def four_units(u, xs, hi, lo):
                for k in range(KT):
                    pe.wait_ge(xs_lo, xs + (k + 1))
                    for j in range(SLOTS):
                        if k == 0:
                            pe.wait_ge(w_lo_done, u + (j + SLOTS + 1))
                        mm = three(j, j, k, hi[:, k, :], lo[:, k, :], k == 0, k == KT - 1)
                        if k == KT - 1:
                            mm.then_inc(pe_unit, 1)

            def mean_square(n):
                pe.wait_ge(ssum_added, n * KT + (KT + 2))
                nc.tensor.matmul(ps[:, STAT, :], mean_d[:], ssum[:], start=True, stop=True).then_inc(stat_ps, 1)

            pe.sem_inc(pe_unit, SLOTS)
            pe.sem_inc(o_ps, 1)
            pe.wait_ge(consts, 1)
            with pe.Fori(0, DEPTH) as l:
                u0, ea, ed, xs = l * UNITS, l * EA, l * ED, l * XS
                mean_square(l * 2)
                four_units(u0, xs + XS_H, h_hi, h_lo)
                with pe.Fori(0, 2) as i:
                    for j in range(SLOTS):
                        pe.wait_ge(evac_act, ea + i * 4 + (EA_V + j + 1))
                        unit(u0 + i * SLOTS + (U_QK + j), j, j, h_hi, h_lo)
                pe.wait_ge(evac_act, ea + (EA_V + HEADS))
                pe.wait_ge(tab_in, 16)
                for h in range(HEADS):
                    for jt in range(T // P):
                        tr = nc.tensor.transpose(ps[:, 4 + h, jt * P:(jt + 1) * P], v_T[:, h, jt * P:(jt + 1) * P], ident)
                    tr.then_inc(v_turned, 1)
                with pe.Fori(0, HEADS) as h:
                    uh = u0 + h * SLOTS + U_HEAD
                    pe.wait_ge(evac_act, ea + h * 2 + (EA_HEAD - 1))
                    unit(uh, 0, 0, h_hi, h_lo)
                    pe.wait_ge(cur_ready, l * HEADS + h + 1)
                    pe.wait_ge(v_centered, l * HEADS + (HEADS + 1))
                    pe.wait_ge(std_ready, l * HEADS + h + 1)
                    for jt in range(T // P):
                        n = T - jt * P
                        mm = nc.tensor.matmul(ps[:, S_BANK[jt], S_COL[jt]:S_COL[jt] + n], k_cur[:, jt * P:(jt + 1) * P],
                                              qkT[:, bass.ds(h * 2, 1), jt * P:T].rearrange("p a t -> p (a t)"),
                                              start=(jt != 3), stop=True, skip_group_check=True)
                        if jt != 2:
                            mm.then_inc(s_ps, 1)
                    pe.wait_ge(evac_act, ea + h * 2 + EA_HEAD)
                    unit(uh + 1, 1, 1, h_hi, h_lo)
                    pe.wait_ge(o_read, l * HEADS + h + 1)
                    for jt in range(T // P):
                        pe.wait_ge(s_ready, l * 16 + h * 4 + (jt + 1))
                        n = T - jt * P
                        mm = nc.tensor.matmul(ps[:, O, jt * P:T], v_cur[:, jt * P:(jt + 1) * P],
                                              s_T[:, S_AT[jt]:S_AT[jt] + n], start=(jt == 0), stop=(jt == 3),
                                              skip_group_check=True)
                    mm.then_inc(o_ps, 1)
                    pe.wait_ge(evac_dve, ed + h * 2 + 1)
                    unit(uh + 2, 2, 2, h_hi, h_lo)
                    pe.wait_ge(osq_ready, l * HEADS + h + 1)
                    nc.tensor.matmul(ps[:, STAT, :], mean_e[:], buf_a[:, 0, :], start=True, stop=True).then_inc(var_ps, 1)
                    pe.wait_ge(evac_dve, ed + h * 2 + 2)
                    unit(uh + 3, 3, 3, h_hi, h_lo)
                four_units(u0 + U_OUT, xs + XS_Y, y_hi, y_lo)
                for j in range(SLOTS):
                    pe.wait_ge(evac_dve, ed + (2 + ED_OUT + j + 1))
                    unit(u0 + (U_OUT + SLOTS + j), j, j, y_hi, y_lo)
                mean_square(l * 2 + 1)
                for half in range(2):
                    if half == 0:
                        four_units(u0 + U_UP[0], xs + XS_H2, h_hi, h_lo)
                    with pe.Fori(1 - half, 4) as i:
                        for j in range(SLOTS):
                            pe.wait_ge(evac_act, ea + i * 4 + (EA_UP[half] - 4 + j + 1))
                            if half and j >= 2:
                                pe.wait_ge(evac_dve, ed + (2 + ED_DOWN[0] + 5 + j))
                            unit(u0 + i * SLOTS + (U_UP[half] + j), j, j, h_hi, h_lo)
                    with pe.Fori(0, 4) as i:
                        for m in range(2):
                            pe.wait_ge(evac_act, ea + (EA_UP[half] + 15 + m))
                            pe.wait_ge(evac_dve, ed + i * 2 + (ED_DOWN[half] + m + 1))
                            for kk in range(2):
                                pe.wait_ge(xs_lo, xs + (XS_U[half] + 8 * (kk + 1)))
                                unit(u0 + i * SLOTS + (U_DOWN[half] + 2 * m + kk), 2 * m + kk, 2 + m, u_hi, u_lo,
                                     k0=8 * kk, first=(kk == 0), last=(kk == 1))
            mean_square(DEPTH * 2)

        @block.scalar
        def _(act):
            def split_hi(l, step, j):
                u = l * UNITS + step * SLOTS + (SLOTS + j)
                act.wait_ge(w_in[j], (l * STEPS + step) * 16 + 32)
                act.wait_ge(pe_unit, u + 1)
                nc.scalar.copy(w_hi[:, j, :], w_raw[:, j, :]).then_inc(w_hi_done, 1)

            def pe_has(l, u):
                act.wait_ge(pe_unit, l * UNITS + u + (SLOTS + 1))

            def norm(l, n, which, xs0):
                act.wait_ge(stat_ps, n + 1)
                nc.scalar.activation(std[:], ps[:, STAT, :], ACT.Sqrt, bias=eps[:, 0:1]).then_inc(norm_std, 1)
                shift = M_SH1 if which == 0 else M_SH2
                for k in range(KT):
                    act.wait_ge(xr_ready, n * KT + (k + 1))
                    if k >= 2:
                        act.wait_ge(xs_lo, l * XS + (xs0 + k - 1))
                    nc.scalar.activation(buf_b[:, k % 2, :], buf_a[:, k % 2, :], ACT.Identity,
                                         scale=gm[:, which, k:k + 1], bias=mod[:, shift + k:shift + k + 1]
                                         ).then_inc(hf_ready, 1)
                    act.wait_ge(hf_ready, n * KT + (k + 1))
                    nc.scalar.copy(h_hi[:, k, :], buf_b[:, k % 2, :]).then_inc(xs_hi, 1)

            def square(n, m, slot, xk):
                act.wait_ge(ssum_added, n * KT + m + 1)
                nc.scalar.activation(buf_a[:, slot, :], xk, ACT.Square).then_inc(sq_ready, 1)

            act.sem_inc(std_ready, 1)
            act.wait_ge(c_in, 16)
            nc.scalar.activation(buf_b[:, :, :].rearrange("p a t -> p (a t)"), c_act[:], ACT.Exp, scale=-1.0
                                 ).then_inc(c_exp, 1)
            act.wait_ge(x_in, 16)
            for m in range(KT):
                square(0, m, m % 2, x[:, m, :])
            act.wait_ge(consts, 1)
            for j in range(SLOTS):
                act.wait_ge(w_in[j], 16)
                nc.scalar.copy(w_hi[:, j, :], w_raw[:, j, :]).then_inc(w_hi_done, 1)

            with act.Fori(0, DEPTH) as l:
                norm(l, l * 2, 0, XS_H)
                for j in range(SLOTS):
                    pe_has(l, U_V + j)
                    nc.scalar.copy(v_T[:, j, :], ps[:, j, :]).then_inc(evac_act, 1)
                    split_hi(l, 0, j)
                with act.Fori(0, 2) as i:
                    for j in range(SLOTS):
                        pe_has(l, i * 4 + (U_QK + j))
                        act.wait_ge(rope_done, l * 8 + i * 4 + (j + 1))
                        nc.scalar.copy(buf_b[0:64, j % 2, :], ps[64:128, j, :])
                        nc.scalar.copy(buf_b[64:128, j % 2, :], ps[0:64, j, :])
                        nc.scalar.copy(buf_a[:, j % 2, :], ps[:, j, :]).then_inc(evac_act, 1)
                        split_hi(l, i + 1, j)
                with act.Fori(0, HEADS) as h:
                    n = l * HEADS + h
                    pe_has(l, h * 4 + U_HEAD)
                    nc.scalar.activation(egr[:], ps[:, 0, :], ACT.Exp, scale=-1.0)
                    nc.scalar.copy(gr[:], ps[:, 0, :]).then_inc(evac_act, 1)
                    split_hi(l, h + 3, 0)
                    pe_has(l, h * 4 + (U_HEAD + 1))
                    nc.scalar.copy(cc[:], ps[:, 1, :]).then_inc(evac_act, 1)
                    split_hi(l, h + 3, 1)
                    act.wait_ge(o_ps, n + 2)
                    nc.scalar.activation(buf_a[:, 0, :], ps[:, O, :], ACT.Square).then_inc(osq_ready, 1)
                    split_hi(l, h + 3, 2)
                    act.wait_ge(var_ps, n + 1)
                    nc.scalar.activation(buf_a[:, 1, :], ps[:, STAT, :], ACT.Sqrt, bias=eps[:, 0:1]).then_inc(std_ready, 1)
                    act.wait_ge(evac_dve, l * ED + h * 2 + (ED_HEAD + 4))
                    nc.scalar.copy(y_hi[:, bass.ds(h * 2, 1), :].rearrange("p a t -> p (a t)"), conv[:]).then_inc(xs_hi, 1)
                    split_hi(l, h + 3, 3)
                    act.wait_ge(gate_step, n * 3 + 3)
                    nc.scalar.copy(y_hi[:, bass.ds(h * 2 + 1, 1), :].rearrange("p a t -> p (a t)"), buf_b[:, 1, :]
                                   ).then_inc(xs_hi, 1)
                for i in range(2):
                    for j in range(SLOTS):
                        m = 4 * i + j
                        act.wait_ge(evac_dve, l * ED + (2 + ED_OUT + m + 1))
                        square(l * 2 + 1, m, m % 2, x[:, m, :])
                        split_hi(l, 7 + i, j)
                norm(l, l * 2 + 1, 1, XS_H2)
                for half in range(2):
                    with act.Fori(0, 4) as i:
                        for j in range(SLOTS):
                            pe_has(l, i * 4 + (U_UP[half] + j))
                            nc.scalar.activation(buf_a[:, j % 2, :], ps[:, j, :], ACT.Relu).then_inc(evac_act, 1)
                            split_hi(l, i + (9 + 8 * half), j)
                            act.wait_ge(rsq_ready, l * 32 + i * 4 + (16 * half + j + 1))
                            nc.scalar.copy(u_hi[:, bass.ds(i * 4 + j, 1), :].rearrange("p a t -> p (a t)"),
                                           buf_b[:, j % 2, :]).then_inc(xs_hi, 1)
                    if half == 0:
                        with act.Fori(0, 4) as i:
                            for j in range(SLOTS):
                                split_hi(l, i + 13, j)

                def down_square(i, m):
                    act.wait_ge(evac_dve, l * ED + i * 2 + (2 + ED_DOWN[1] + m + 1))
                    square(l * 2 + 2, i * 2 + m, m, x[:, bass.ds(i * 2 + m, 1), :].rearrange("p a t -> p (a t)"))

                with act.Fori(0, 3) as i:
                    for m in range(2):
                        split_hi(l, i + 21, 2 * m)
                        down_square(i, m)
                        split_hi(l, i + 21, 2 * m + 1)
                for m in range(2):
                    with act.If(l < DEPTH - 1):
                        split_hi(l, 24, 2 * m)
                    down_square(3, m)
                    with act.If(l < DEPTH - 1):
                        split_hi(l, 24, 2 * m + 1)
            act.wait_ge(stat_ps, 2 * DEPTH + 1)
            nc.scalar.activation(std[:], ps[:, STAT, :], ACT.Sqrt, bias=eps[:, 0:1]).then_inc(norm_std, 1)

        @block.vector
        def _(dve):
            def split_lo(l, step, j):
                dve.wait_ge(w_hi_done, l * UNITS + step * SLOTS + (SLOTS + j + 1))
                nc.vector.tensor_tensor(w_lo[:, j, :], w_raw[:, j, :], w_hi[:, j, :].bitcast(F32), ALU.subtract
                                        ).then_inc(w_lo_done, 1)

            def pe_has(l, u):
                dve.wait_ge(pe_unit, l * UNITS + u + (SLOTS + 1))

            def reduce_ada(pair, j):
                dve.wait_ge(ada_in[j], pair * 16 + 16)
                if j == 0:
                    dve.wait_ge(mod_added, pair + KT)
                nc.vector.tensor_tensor_reduce(out=ada_raw[:, j, :], in0=ada_raw[:, j, :], in1=c_act[:],
                                               scale=1.0, scalar=0.0, op0=ALU.mult, op1=ALU.add,
                                               accum_out=ada_sum[:, j:j + 1]).then_inc(ada_done, 1)

            def add_bias(pair, col):
                dve.wait_ge(ada_done, pair * 2 + 4)
                nc.vector.tensor_tensor(mod[:, bass.ds(col, 2)], ada_sum[:], bia[:, bass.ds(below(pair * 2 + FIRST_MODS, DEPTH * MODS, 2), 2)],
                                        ALU.add).then_inc(mod_added, 1)

            def xs_low(l, i, out, full, hi):
                dve.wait_ge(xs_hi, l * XS + i + 1)
                nc.vector.tensor_tensor(out, full, hi.bitcast(F32), ALU.subtract).then_inc(xs_lo, 1)

            def norm_scale(n):
                dve.wait_ge(norm_std, n + 1)
                nc.vector.reciprocal(rinv[:], std[:]).then_inc(norm_r, 1)
                dve.wait_ge(norm_r, n + 1)

            def norm(l, n, which, xs0, g_col, scale_col):
                nc.vector.scalar_tensor_tensor(out=gm[:, which, :], in0=mod[:, scale_col:scale_col + KT], scalar=1.0,
                                               in1=par[:, bass.ds(l * PARAMS + g_col, KT)], op0=ALU.add, op1=ALU.mult
                                               ).then_inc(gm_ready, 1)
                norm_scale(n)
                for k in range(KT + 1):
                    if k < KT:
                        nc.vector.tensor_tensor(buf_a[:, k % 2, :], x[:, k, :], rinv[:], ALU.mult).then_inc(xr_ready, 1)
                    if k >= 1:
                        xs_low(l, xs0 + k - 1, h_lo[:, k - 1, :], buf_b[:, (k - 1) % 2, :], h_hi[:, k - 1, :])

            def residual(m, bank, gate_col):
                xm = x[:, bass.ds(m, 1), :].rearrange("p a t -> p (a t)")
                nc.vector.scalar_tensor_tensor(out=xm, in0=ps[:, bank, :], scalar=mod[:, bass.ds(m + gate_col, 1)],
                                               in1=xm, op0=ALU.mult, op1=ALU.add).then_inc(evac_dve, 1)

            dve.sem_inc(w_lo_done, SLOTS)
            dve.sem_inc(ada_done, 2)
            dve.sem_inc(evac_dve, 2)
            for s in (v_centered, o_read, conv_step):
                dve.sem_inc(s, 1)
            nc.vector.memset(eps[:], EPS)
            nc.vector.memset(z[:], 0.0)
            nc.vector.memset(mean_d[:], 1.0 / D)
            nc.vector.memset(mean_e[:], 1.0 / P).then_inc(consts, 1)
            c_tmp = buf_b[:, :, :].rearrange("p a t -> p (a t)")
            dve.wait_ge(c_exp, 1)
            nc.vector.tensor_scalar(c_tmp, c_tmp, 1.0, None, ALU.add).then_inc(c_step, 1)
            dve.wait_ge(c_step, 1)
            nc.vector.reciprocal(c_tmp, c_tmp).then_inc(c_step, 1)
            dve.wait_ge(c_step, 2)
            nc.vector.tensor_tensor(c_act[:], c_act[:], c_tmp, ALU.mult).then_inc(c_step, 1)
            dve.wait_ge(c_step, 3)
            dve.wait_ge(par_in, 48)
            for m in range(FIRST_MODS):
                dve.wait_ge(ada0_in[m // 4], 16)
                if m % 2 == 0 and m:
                    dve.wait_ge(mod_added, m // 2)
                nc.vector.tensor_tensor_reduce(out=arena[:, m, :], in0=arena[:, m, :], in1=c_act[:],
                                               scale=1.0, scalar=0.0, op0=ALU.mult, op1=ALU.add,
                                               accum_out=ada_sum[:, m % 2:m % 2 + 1]).then_inc(ada0_done, 1)
                if m % 2:
                    dve.wait_ge(ada0_done, m + 1)
                    nc.vector.tensor_tensor(mod[:, m - 1:m + 1], ada_sum[:], bia[:, m - 1:m + 1], ALU.add
                                            ).then_inc(mod_added, 1)
            for j in range(SLOTS):
                dve.wait_ge(w_hi_done, j + 1)
                nc.vector.tensor_tensor(w_lo[:, j, :], w_raw[:, j, :], w_hi[:, j, :].bitcast(F32), ALU.subtract
                                        ).then_inc(w_lo_done, 1)
            dve.wait_ge(x_in, 16)
            dve.wait_ge(tab_in, 16)

            with dve.Fori(0, DEPTH) as l:
                pair0 = l * (MODS // 2)
                dve.wait_ge(mod_added, l * 24 + 8)
                norm(l, l * 2, 0, XS_H, C_G1, M_SC1)
                for j in range(SLOTS):
                    split_lo(l, 0, j)
                with dve.Fori(0, 2) as i:
                    for j in range(SLOTS):
                        split_lo(l, i + 1, j)
                        reduce_ada(pair0 + i * 2 + j // 2, j % 2)
                        if j % 2:
                            add_bias(pair0 + i * 2 + j // 2, i * 4 + (FIRST_MODS + j - 1))
                for h in range(HEADS):
                    dve.wait_ge(v_turned, l * HEADS + (h + 1))
                    dve.wait_ge(v_centered, l * HEADS + (h + 1))
                    vp = ps[:, 4 + h, :].rearrange("p (j e) -> p j e", e=P)
                    nc.vector.tensor_reduce(vsum[:], vp, AX_X, ALU.add).then_inc(v_summed, 1)
                    dve.wait_ge(v_summed, l * HEADS + (h + 1))
                    nc.vector.scalar_tensor_tensor(
                        out=v_tok[:, h, :].rearrange("p (j e) -> p j e", e=P),
                        in0=vsum[:].unsqueeze(2).to_broadcast([P, T // P, P]), scalar=-1.0 / P, in1=vp,
                        op0=ALU.mult, op1=ALU.add).then_inc(v_centered, 1)
                with dve.Fori(0, HEADS) as h:
                    n = l * HEADS + h

                    def ada_in_step(j):
                        reduce_ada(pair0 + h * 2 + (4 + j // 2), j % 2)
                        if j % 2:
                            add_bias(pair0 + h * 2 + (4 + j // 2), h * 4 + (FIRST_MODS + 8 + j - 1))

                    split_lo(l, h + 3, 0)
                    ada_in_step(0)
                    for jt in range(T // P):
                        if jt != 3:
                            dve.wait_ge(s_ps, n * 3 + (jt + 1))
                        w = T - jt * P
                        nc.vector.tensor_tensor(s_T[:, S_AT[jt]:S_AT[jt] + w],
                                                ps[:, S_BANK[jt], S_COL[jt]:S_COL[jt] + w],
                                                decay[:, bass.ds(h, 1), 0:w].rearrange("p a t -> p (a t)"), ALU.mult
                                                ).then_inc(s_ready, 1)
                    split_lo(l, h + 3, 1)
                    ada_in_step(1)
                    pe_has(l, h * 4 + (U_HEAD + 2))
                    dve.wait_ge(evac_act, l * EA + h * 2 + (EA_HEAD + 2))
                    dve.wait_ge(conv_step, n * 3 + 1)
                    nc.vector.tensor_tensor(z[:, 2:T + 2], ps[:, 2, :], cc[:], ALU.mult).then_inc(evac_dve, 1)
                    split_lo(l, h + 3, 2)
                    tap = [par[:, bass.ds(l * PARAMS + h * 3 + (C_CONV + t), 1)] for t in range(3)]
                    dve.wait_ge(evac_dve, l * ED + h * 2 + (2 + ED_HEAD + 1))
                    dve.wait_ge(xs_lo, l * XS + h * 2 + XS_Y)
                    nc.vector.tensor_scalar(conv[:], z[:, 0:T], tap[0], None, ALU.mult).then_inc(conv_step, 1)
                    for t in (1, 2):
                        dve.wait_ge(conv_step, n * 3 + (t + 1))
                        nc.vector.scalar_tensor_tensor(out=conv[:], in0=z[:, t:t + T], scalar=tap[t], in1=conv[:],
                                                       op0=ALU.mult, op1=ALU.add).then_inc(conv_step, 1)
                    ada_in_step(2)
                    dve.wait_ge(var_ps, n + 1)
                    nc.vector.scalar_tensor_tensor(out=buf_b[:, 1, :], in0=ps[:, O, :],
                                                   scalar=par[:, bass.ds(l * PARAMS + h + C_RET, 1)], in1=gr[:],
                                                   op0=ALU.mult, op1=ALU.mult).then_inc(o_read, 1)
                    ada_in_step(3)
                    pe_has(l, h * 4 + (U_HEAD + 3))
                    dve.wait_ge(conv_step, n * 3 + 4)
                    nc.vector.tensor_tensor(conv[:], ps[:, 3, :], conv[:], ALU.mult).then_inc(evac_dve, 1)
                    dve.wait_ge(std_ready, n + 2)
                    nc.vector.scalar_tensor_tensor(out=egr[:], in0=egr[:], scalar=1.0, in1=buf_a[:, 1, :],
                                                   op0=ALU.add, op1=ALU.mult).then_inc(gate_step, 1)
                    xs_low(l, h * 2 + XS_Y, y_lo[:, bass.ds(h * 2, 1), :].rearrange("p a t -> p (a t)"), conv[:],
                           y_hi[:, bass.ds(h * 2, 1), :].rearrange("p a t -> p (a t)"))
                    split_lo(l, h + 3, 3)
                    dve.wait_ge(gate_step, n * 3 + 1)
                    nc.vector.reciprocal(buf_b[:, 0, :], egr[:]).then_inc(gate_step, 1)
                    dve.wait_ge(gate_step, n * 3 + 2)
                    nc.vector.tensor_tensor(buf_b[:, 1, :], buf_b[:, 1, :], buf_b[:, 0, :], ALU.mult
                                            ).then_inc(gate_step, 1)
                    xs_low(l, h * 2 + (XS_Y + 1), y_lo[:, bass.ds(h * 2 + 1, 1), :].rearrange("p a t -> p (a t)"),
                           buf_b[:, 1, :], y_hi[:, bass.ds(h * 2 + 1, 1), :].rearrange("p a t -> p (a t)"))
                dve.wait_ge(mod_added, l * 24 + 20)
                for i in range(2):
                    for j in range(SLOTS):
                        pe_has(l, U_OUT + 4 * i + j)
                        residual(4 * i + j, j, M_GATE1)
                        split_lo(l, 7 + i, j)
                norm(l, l * 2 + 1, 1, XS_H2, C_G2, M_SC2)
                for half in range(2):
                    with dve.Fori(0, 4) as i:
                        for j in range(SLOTS):
                            split_lo(l, i + (9 + 8 * half), j)
                            ub = bass.ds(i * 4 + j, 1)
                            xs_low(l, i * 4 + (XS_U[half] + j), u_lo[:, ub, :].rearrange("p a t -> p (a t)"),
                                   buf_b[:, j % 2, :], u_hi[:, ub, :].rearrange("p a t -> p (a t)"))
                            if half == 0 and j < 2:
                                reduce_ada(pair0 + i + 12, j)
                        if half == 0:
                            add_bias(pair0 + i + 12, i * 2 + M_GATE2)
                        else:
                            with dve.If(l < DEPTH - 1):
                                for j in range(2):
                                    reduce_ada(pair0 + i + 20, j)
                                add_bias(pair0 + i + 20, i * 2 + KT)
                    if half == 0:
                        with dve.Fori(0, 4) as i:
                            for m in range(2):
                                split_lo(l, i + 13, 2 * m)
                                pe_has(l, i * 4 + (U_DOWN[0] + 2 * m + 1))
                                dve.wait_ge(mod_added, l * 24 + 24)
                                residual(i * 2 + m, 2 + m, M_GATE2)
                                split_lo(l, i + 13, 2 * m + 1)
                            with dve.If(l < DEPTH - 1):
                                for j in range(2):
                                    reduce_ada(pair0 + i + 16, j)
                                add_bias(pair0 + i + 16, i * 2)
                    else:
                        with dve.Fori(0, 3) as i:
                            for m in range(2):
                                split_lo(l, i + 21, 2 * m)
                                pe_has(l, i * 4 + (U_DOWN[1] + 2 * m + 1))
                                residual(i * 2 + m, 2 + m, M_GATE2)
                                split_lo(l, i + 21, 2 * m + 1)
                        for m in range(2):
                            with dve.If(l < DEPTH - 1):
                                split_lo(l, 24, 2 * m)
                            pe_has(l, U_DOWN[1] + 12 + 2 * m + 1)
                            residual(6 + m, 2 + m, M_GATE2)
                            with dve.If(l < DEPTH - 1):
                                split_lo(l, 24, 2 * m + 1)
            norm_scale(2 * DEPTH)
            for k in range(KT):
                nc.vector.scalar_tensor_tensor(out=x[:, k, :], in0=x[:, k, :], scalar=fin_g[:, k:k + 1], in1=rinv[:],
                                               op0=ALU.mult, op1=ALU.mult).then_inc(out_ready, 1)

        @block.gpsimd
        def _(pool):
            def clear_sum(n):
                if not (isinstance(n, int) and n == 0):
                    pool.wait_ge(stat_ps, n)
                else:
                    pool.wait_ge(consts, 1)
                zero = z[:, 0:1].to_broadcast([P, T])
                nc.gpsimd.tensor_tensor(ssum[:], zero, zero, ALU.add).then_inc(ssum_clear, 1)

            def add_square(n, m, slot):
                pool.wait_ge(sq_ready, n * KT + m + 1)
                pool.wait_ge(ssum_clear, n + 1)
                pool.wait_ge(ssum_added, n * KT + m + 2)
                nc.gpsimd.tensor_tensor(ssum[:], ssum[:], buf_a[:, slot, :], ALU.add).then_inc(ssum_added, 1)

            pool.sem_inc(ssum_added, 2)
            pool.sem_inc(rope_done, 2)
            clear_sum(0)
            for m in range(KT):
                add_square(0, m, m % 2)
            pool.wait_ge(tab_in, 16)
            with pool.Fori(0, DEPTH) as l:
                with pool.Fori(0, 2) as i:
                    for j in range(SLOTS):
                        n = l * 8 + i * 4 + j
                        a, b = buf_a[:, j % 2, :], buf_b[:, j % 2, :]
                        pool.wait_ge(evac_act, l * EA + i * 4 + (EA_QK + j + 1))
                        nc.gpsimd.tensor_tensor(a, a, cos, ALU.mult)
                        nc.gpsimd.tensor_tensor(b, b, sin, ALU.mult).then_inc(rope_step, 1)
                        pool.wait_ge(rope_step, n + 1)
                        nc.gpsimd.tensor_tensor(qkT[:, bass.ds(i * 4 + j, 1), :].rearrange("p a t -> p (a t)"), a, b,
                                                ALU.add).then_inc(rope_done, 1)
                with pool.Fori(0, HEADS) as h:
                    n = l * HEADS + h
                    pool.wait_ge(o_ps, n + 1)
                    pool.wait_ge(rope_done, l * 8 + 10)
                    nc.gpsimd.tensor_copy(k_cur[:], qkT[:, bass.ds(h * 2 + 1, 1), :].rearrange("p a t -> p (a t)"))
                    pool.wait_ge(v_centered, n + 2)
                    nc.gpsimd.tensor_copy(v_cur[:], v_tok[:, bass.ds(h, 1), :].rearrange("p a t -> p (a t)")
                                          ).then_inc(cur_ready, 1)
                pool.wait_ge(evac_dve, l * ED + (2 + ED_OUT + 1))
                clear_sum(l * 2 + 1)
                for m in range(KT):
                    add_square(l * 2 + 1, m, m % 2)
                for half in range(2):
                    with pool.Fori(0, 4) as i:
                        for j in range(SLOTS):
                            pool.wait_ge(evac_act, l * EA + i * 4 + (EA_UP[half] + j + 1))
                            pool.wait_ge(xs_lo, l * XS + i * 4 + (XS_U[half] + j - 1))
                            nc.gpsimd.tensor_tensor(buf_b[:, j % 2, :], buf_a[:, j % 2, :], buf_a[:, j % 2, :], ALU.mult
                                                    ).then_inc(rsq_ready, 1)
                clear_sum(l * 2 + 2)
                with pool.Fori(0, 4) as i:
                    for m in range(2):
                        add_square(l * 2 + 2, i * 2 + m, m)


def shape_tables():
    import numpy as np
    decay = np.zeros((HEADS, P, T), np.float64)
    off = np.arange(T)[None, :] - np.arange(P)[:, None]
    for h in range(HEADS):
        log_g = np.log1p(-np.exp2(-5.0 - h))
        decay[h] = np.where(off >= 0, np.exp(log_g * np.maximum(off, 0)), 0.0) * P ** -0.5
    half = P // 2
    inv = np.float32(10000.0) ** (-np.arange(0, P, 2, dtype=np.float32) / np.float32(P))
    ang = inv[:, None] * np.arange(T, dtype=np.float32)[None, :]
    cos = np.concatenate([np.cos(ang), np.cos(ang)])
    sin = np.concatenate([-np.sin(ang), np.sin(ang)])
    assert cos.shape == (2 * half, T)
    parts = [decay.transpose(1, 0, 2).reshape(P, HEADS * T), cos, sin, np.eye(P)]
    return np.ascontiguousarray(np.concatenate([p.astype(np.float32) for p in parts], axis=1))


def columns(w):
    k, n = w.shape
    return w.reshape(k // P, P, n // P, P).transpose(2, 0, 1, 3)


def weight_stream(w_in, w_out, w_up, w_down):
    import numpy as np
    units = []
    for l in range(DEPTH):
        t = columns(w_in[l])
        cb, ccs, cu, q, k, v, g = (t[4 * i:4 * i + 4] for i in range(7))
        units += list(v)
        for h in range(HEADS):
            units += [q[h], k[h]]
        for h in range(HEADS):
            units += [g[h], ccs[h], cu[h], cb[h]]
        order = [half * HEADS + h for h in range(HEADS) for half in range(2)]
        units += list(columns(w_out[l])[:, order])
        up, down = columns(w_up[l]), columns(w_down[l])
        for half in range(2):
            units += list(up[half * HALF_TILES:(half + 1) * HALF_TILES])
            for m in range(KT):
                for kk in range(2):
                    k0 = half * HALF_TILES + 8 * kk
                    units.append(down[m, k0:k0 + 8])
    out = np.empty((len(units), P, KT, P), np.float32)
    for i, u in enumerate(units):
        out[i] = u.transpose(1, 0, 2)
    return out.reshape(len(units), P, D)


def kernel(x, c, norm1_g, w_in, conv_w, ret_norm_g, w_out, norm2_g, w_up, w_down, w_ada, b_ada, final_g):
    import numpy as np
    import concourse.bacc as bacc
    from concourse.bass_utils import run_bass_kernel_spmd

    cols = lambda a: np.asarray(a).reshape(-1, P).T
    params = []
    for l in range(DEPTH):
        params += [cols(norm1_g[l]), cols(norm2_g[l]),
                   np.asarray(conv_w[l]).reshape(3, HEADS, P).transpose(2, 1, 0).reshape(P, 12), cols(ret_norm_g[l])]
    arrays = {
        "xT": np.asarray(x)[0].T.reshape(KT, P, T),
        "c_rows": np.broadcast_to(np.asarray(c).reshape(1, D), (P, D)),
        "weights": weight_stream(*(np.asarray(w) for w in (w_in, w_out, w_up, w_down))),
        "ada": np.asarray(w_ada).transpose(0, 2, 1).reshape(DEPTH * MODS, P, D),
        "params": np.concatenate(params, axis=1),
        "bias": cols(b_ada),
        "final_g": cols(final_g),
        "tables": shape_tables(),
    }
    arrays = {k: np.ascontiguousarray(v) for k, v in arrays.items()}
    nc = bacc.Bacc("TRN2", target_bir_lowering=False, num_devices=1)
    aps = {k: nc.dram_tensor(k, v.shape, mybir.dt.from_np(v.dtype), kind="ExternalInput").ap()
           for k, v in arrays.items()}
    outT = nc.dram_tensor("outT", (KT, P, T), F32, kind="ExternalOutput").ap()
    trunk(nc, **aps, outT=outT)
    result = run_bass_kernel_spmd(nc, [arrays], core_ids=[0])
    return np.ascontiguousarray(result.results[0]["outT"].reshape(D, T).T).reshape(1, T, D)
```

```python
from contextlib import ExitStack

import concourse.bass as bass
from concourse import mybir

P = 128
D = 1024
T = 512
DEPTH = 2
KT = D // P
HEADS = 4
EPS = 1e-6
SLOTS = 4
UNITS = 100
STEPS = UNITS // SLOTS
MODS = 6 * KT
TOKEN_TILES = T // P
ADDED = KT - 1
FIRST_MODS = 2 * KT
HALF_TILES = 16

U_V, U_QK, U_HEAD, U_OUT = 0, 4, 12, 28
U_UP = (36, 68)
U_DOWN = (52, 84)
EA_V, EA_QK, EA_HEAD, EA_UP = 0, 4, 12, (20, 36)
EA = 52
ED_HEAD, ED_OUT, ED_DOWN = 0, 8, (16, 24)
ED = 32
XS_H, XS_Y, XS_H2, XS_U = 0, 8, 16, (24, 40)
XS = 56
C_G1, C_G2, C_CONV, C_RET = 0, 8, 16, 28
PARAMS = 32
M_GATE1, M_SH2, M_SC2, M_GATE2 = range(2 * KT, MODS, KT)

F32 = mybir.dt.float32
F32R = mybir.dt.float32r
ALU = mybir.AluOpType
ACT = mybir.ActivationFunctionType
AX_X = mybir.AxisListType.X


def trunk(nc, xT, c_cols, weights, ada, params, bias, final_g, identity, tables, outT):
    with ExitStack() as ctx:
        def sb(name, shape, dt=F32):
            return ctx.enter_context(nc.sbuf_tensor(name, shape, dt))

        def sem(name):
            return ctx.enter_context(nc.semaphore(name))

        arena_at = -(-nc.sbuf_base // 32) * 32
        arena = sb("arena", [P, 16, D])
        over = [arena_at]

        def view(name, shape, dt=F32):
            size = 4
            for n in shape[1:]:
                size *= n
            t = nc.alloc_sbuf_tensor_at(name, shape, dt, offset=over[0])
            over[0] += size
            assert over[0] <= arena_at + 16 * D * 4
            return t

        u_hi = view("u_hi", [P, HALF_TILES, T], F32R)
        u_lo = view("u_lo", [P, HALF_TILES, T], F32R)
        over[0] = arena_at
        y_hi = view("y_hi", [P, KT, T], F32R)
        qk_at = over[0]
        qkT = view("qkT", [P, 2 * HEADS, T])
        v_T = view("v_T", [P, HEADS, T])
        v_tok = view("v_tok", [P, HEADS, T])
        conv = v_T[:, 0, :]
        cc = v_T[:, 1, :]
        k_cur = view("k_cur", [P, T])
        v_cur = view("v_cur", [P, T])
        s_T = view("s_T", [P, 1280])
        gr = view("gr", [P, T])
        egr = view("egr", [P, T])
        over[0] = qk_at
        y_lo = view("y_lo", [P, KT, T], F32R)

        x = sb("x", [P, KT, T])
        h_hi = sb("h_hi", [P, KT, T], F32R)
        h_lo = sb("h_lo", [P, KT, T], F32R)
        w_raw = sb("w_raw", [P, SLOTS, D])
        w_hi = sb("w_hi", [P, SLOTS, D], F32R)
        w_lo = sb("w_lo", [P, SLOTS, D], F32R)
        ada_raw = sb("ada_raw", [P, SLOTS, D])
        tab = sb("tab", [P, tables.shape[1]])
        decay = tab[:, 0:HEADS * T].rearrange("p (h t) -> p h t", h=HEADS)
        cos = tab[:, HEADS * T:HEADS * T + T]
        sin = tab[:, HEADS * T + T:HEADS * T + 2 * T]
        ident = sb("ident", [P, P])
        c_col = sb("c_col", [P, 2, KT])
        c_act = sb("c_act", [P, D])
        par = sb("par", [P, DEPTH * PARAMS])
        bia = sb("bia", [P, DEPTH * MODS])
        fin_g = sb("fin_g", [P, KT])
        mod = sb("mod", [P, MODS])
        ada_sum = sb("ada_sum", [P, 2])
        gm = sb("gm", [P, 2, KT])
        eps = sb("eps", [P, 1])
        vsum = sb("vsum", [P, HEADS])
        ones = sb("ones", [P, P])
        mean_d = sb("mean_d", [P, 1])
        mean_e = sb("mean_e", [P, P])
        buf_a = sb("buf_a", [P, 2, T])
        buf_b = sb("buf_b", [P, 2, T])
        ring = [buf_a[:, 0, :], buf_a[:, 1, :], buf_b[:, 0, :], buf_b[:, 1, :]]
        ssum = sb("ssum", [P, T])
        std = sb("std", [P, TOKEN_TILES])
        rstd = sb("rstd", [P, TOKEN_TILES])
        z = sb("z", [P, T + 2])

        ps = ctx.enter_context(nc.psum_tensor("ps", [P, 8, T], F32))
        S_BANK = (4, 5, 6, 6)
        S_COL = (0, 0, 0, 256)
        S_AT = (0, 512, 896, 1152)
        STAT, RMS, O = 4, 5, 7
        OUT_BANK = (6, 7, 0, 1)
        rinv = ps[:, RMS, :]

        c_in, par_in, tab_in = sem("c_in"), sem("par_in"), sem("tab_in")
        x_in = [sem(f"x_in{i}") for i in range(2)]
        ada0_in = [sem(f"ada0_in{i}") for i in range(KT)]
        w_in = [sem(f"w_in{i}") for i in range(SLOTS)]
        ada_in = [sem(f"ada_in{i}") for i in range(SLOTS)]
        consts = sem("consts")
        c_exp, c_step, c_ps, c_ready = sem("c_exp"), sem("c_step"), sem("c_ps"), sem("c_ready")
        w_hi_done = sem("w_hi_done")
        w_lo_done = sem("w_lo_done")
        pe_unit = sem("pe_unit")
        ada_done = sem("ada_done")
        ada0_done = sem("ada0_done")
        mod_added = sem("mod_added")
        evac_act = sem("evac_act")
        evac_dve = sem("evac_dve")
        xs_hi, xs_lo = sem("xs_hi"), sem("xs_lo")
        sq_ready = sem("sq_ready")
        ssum_added = sem("ssum_added")
        ssum_clear = sem("ssum_clear")
        stat_ps, norm_std, norm_r, rinv_ps = sem("stat_ps"), sem("norm_std"), sem("norm_r"), sem("rinv_ps")
        gm_ready = sem("gm_ready")
        xr_ready, hf_ready = sem("xr_ready"), sem("hf_ready")
        rope_step = sem("rope_step")
        rope_done = sem("rope_done")
        v_turned, v_summed = sem("v_turned"), sem("v_summed")
        v_centered = sem("v_centered")
        cur_ready, s_ps, s_ready = sem("cur_ready"), sem("s_ps"), sem("s_ready")
        o_ps, o_read, std_ready = sem("o_ps"), sem("o_read"), sem("std_ready")
        osq_ready, var_ps = sem("osq_ready"), sem("var_ps")
        conv_step = sem("conv_step")
        gate_step = sem("gate_step")
        rsq_ready = sem("rsq_ready")
        out_ready, out_done = sem("out_ready"), sem("out_done")

        block = ctx.enter_context(nc.Block())

        def below(value, limit, size=1):
            return nc.s_assert_within(value, 0, limit - size,
                                      skip_runtime_bounds_check_because="under If(l < DEPTH - 1)")

        @block.sync
        def _(sp):
            def load_weight(l, step, j):
                u = l * UNITS + step * SLOTS + (SLOTS + j)
                sp.wait_ge(w_lo_done, u + 1)
                sp.dma_start(w_raw[:, j, :], weights[bass.ds(below(u, DEPTH * UNITS), 1), :, :].rearrange("a p n -> p (a n)")
                             ).then_inc(w_in[j], 16)

            def load_ada(b, slot, since):
                sp.wait_ge(ada_done, b + (SLOTS - since + 1))
                sp.dma_start(ada_raw[:, slot, :],
                             ada[bass.ds(below(b + FIRST_MODS, DEPTH * MODS), 1), :, :].rearrange("a p n -> p (a n)")
                             ).then_inc(ada_in[slot], 16)

            def load_step(l, step, adas, b, since=SLOTS):
                for j in range(SLOTS):
                    load_weight(l, step, j)
                    for a in range(j * adas // SLOTS, (j + 1) * adas // SLOTS):
                        load_ada(b + a, a % since, since)

            sp.dma_start(c_col[:, 0, :], c_cols).then_inc(c_in, 16)
            sp.dma_start(ident[:], identity).then_inc(c_in, 16)
            for i in range(2):
                sp.dma_start(x[:, 4 * i:4 * i + 4, :], xT[4 * i:4 * i + 4, :, :].rearrange("k p t -> p k t")
                             ).then_inc(x_in[i], 16)
            sp.dma_start(par[:], params).then_inc(par_in, 16)
            sp.dma_start(bia[:], bias).then_inc(par_in, 16)
            sp.dma_start(fin_g[:], final_g).then_inc(par_in, 16)
            for i in range(KT):
                sp.dma_start(arena[:, 2 * i:2 * i + 2, :], ada[2 * i:2 * i + 2, :, :].rearrange("a p n -> p a n")
                             ).then_inc(ada0_in[i], 16)
                if i == 0:
                    for j in range(SLOTS):
                        sp.dma_start(w_raw[:, j, :], weights[j, :, :]).then_inc(w_in[j], 16)
            sp.dma_start(tab[:], tables).then_inc(tab_in, 16)

            with sp.Fori(0, DEPTH) as l:
                b0 = l * MODS
                with sp.Fori(0, 2) as i:
                    load_step(l, i, 4, b0 + i * 4)
                load_step(l, 2, 8, b0 + 8)
                with sp.Fori(0, HEADS) as i:
                    load_step(l, i + 3, 2, b0 + i * 2 + 16, since=2)
                with sp.Fori(0, 2) as i:
                    load_step(l, i + 7, 0, 0)
                with sp.Fori(0, 4) as i:
                    load_step(l, i + 9, 2, b0 + i * 2 + 24, since=2)
                with sp.Fori(0, 8) as i:
                    load_weight(l, i + 13, 0)
                    load_weight(l, i + 13, 1)
                    with sp.If(l < DEPTH - 1):
                        for a in range(2):
                            load_ada(b0 + i * 2 + (32 + a), a, 2)
                    load_weight(l, i + 13, 2)
                    load_weight(l, i + 13, 3)
                with sp.Fori(0, 3) as i:
                    load_step(l, i + 21, 0, 0)
                with sp.If(l < DEPTH - 1):
                    load_step(l, 24, 0, 0)

            for k in range(KT):
                sp.wait_ge(out_ready, k + 1)
                sp.dma_start(outT[k, :, :], x[:, k, :]).then_inc(out_done, 16)
            sp.wait_ge(out_done, 16 * KT)

        @block.tensor
        def _(pe):
            def three(bank, j, k, hi, lo, first, last):
                wh, wl = w_hi[:, j, k * P:(k + 1) * P], w_lo[:, j, k * P:(k + 1) * P]
                nc.tensor.matmul(ps[:, bank, :], wh, hi, start=first, stop=False)
                nc.tensor.matmul(ps[:, bank, :], wh, lo, start=False, stop=False)
                return nc.tensor.matmul(ps[:, bank, :], wl, hi, start=False, stop=last)

            def unit(u, j, bank, hi, lo, k0=0, first=True, last=True):
                pe.wait_ge(w_lo_done, u + (SLOTS + 1))
                for k in range(KT):
                    mm = three(bank, j, k, hi[:, k0 + k, :], lo[:, k0 + k, :], first and k == 0, last and k == KT - 1)
                mm.then_inc(pe_unit, 1)

            def four_units(u, xs, hi, lo, together):
                for k in range(together):
                    pe.wait_ge(xs_lo, xs + (k + 1))
                    for j in range(SLOTS):
                        if k == 0:
                            pe.wait_ge(w_lo_done, u + (j + SLOTS + 1))
                        three(j, j, k, hi[:, k, :], lo[:, k, :], k == 0, False)
                for j in range(SLOTS):
                    for k in range(together, KT):
                        if j == 0:
                            pe.wait_ge(xs_lo, xs + (k + 1))
                        mm = three(j, j, k, hi[:, k, :], lo[:, k, :], False, k == KT - 1)
                    mm.then_inc(pe_unit, 1)

            def rms(n):
                pe.wait_ge(ssum_added, n * ADDED + (ADDED + 2))
                for part, squares in enumerate((ssum[:], buf_a[:, 1, :])):
                    if part:
                        pe.wait_ge(sq_ready, n * KT + KT)
                    for t in range(TOKEN_TILES):
                        mm = nc.tensor.matmul(ps[:, STAT, t:t + 1], squares[:, t * P:(t + 1) * P], mean_d[:],
                                              start=(part == 0 and t == 0), stop=(part == 1), skip_group_check=True)
                mm.then_inc(stat_ps, 1)
                pe.wait_ge(norm_r, n * 2 + 2)
                nc.tensor.matmul(rinv, ones[:], ssum[:], start=True, stop=True).then_inc(rinv_ps, 1)

            pe.sem_inc(pe_unit, SLOTS)
            pe.sem_inc(o_ps, 1)
            pe.wait_ge(consts, 1)
            pe.wait_ge(c_step, 4)
            for i in range(2):
                nc.tensor.matmul(ps[:, i, :], ones[:], ada_raw[:, 0, i * T:(i + 1) * T], start=True, stop=True
                                 ).then_inc(c_ps, 1)
            rms(0)
            pe.wait_ge(c_ready, 2)
            with pe.Fori(0, DEPTH) as l:
                u0, ea, ed, xs = l * UNITS, l * EA, l * ED, l * XS
                four_units(u0, xs + XS_H, h_hi, h_lo, 4)
                for j in range(2 * SLOTS):
                    pe.wait_ge(evac_act, ea + (EA_V + j + 1))
                    unit(u0 + (U_QK + j), j % SLOTS, j % SLOTS, h_hi, h_lo)
                    if j == 0:
                        pe.wait_ge(evac_act, ea + (EA_V + HEADS))
                        for h in range(HEADS):
                            for jt in range(TOKEN_TILES):
                                tr = nc.tensor.transpose(ps[:, 4 + h, jt * P:(jt + 1) * P],
                                                         v_T[:, h, jt * P:(jt + 1) * P], ident[:])
                            tr.then_inc(v_turned, 1)
                with pe.Fori(0, HEADS) as h:
                    uh = u0 + h * SLOTS + U_HEAD
                    pe.wait_ge(evac_act, ea + h * 2 + (EA_HEAD - 1))
                    unit(uh, 0, 0, h_hi, h_lo)
                    pe.wait_ge(cur_ready, l * HEADS + h + 1)
                    pe.wait_ge(v_centered, l * HEADS + (HEADS + 1))
                    pe.wait_ge(std_ready, l * HEADS + h + 1)
                    for jt in range(TOKEN_TILES):
                        n = T - jt * P
                        mm = nc.tensor.matmul(ps[:, S_BANK[jt], S_COL[jt]:S_COL[jt] + n], k_cur[:, jt * P:(jt + 1) * P],
                                              qkT[:, bass.ds(h * 2, 1), jt * P:T].rearrange("p a t -> p (a t)"),
                                              start=(jt != 3), stop=True, skip_group_check=True)
                        if jt != 2:
                            mm.then_inc(s_ps, 1)
                    pe.wait_ge(evac_act, ea + h * 2 + EA_HEAD)
                    unit(uh + 1, 1, 1, h_hi, h_lo)
                    pe.wait_ge(o_read, l * HEADS + h + 1)
                    for jt in range(TOKEN_TILES):
                        pe.wait_ge(s_ready, l * 16 + h * 4 + (jt + 1))
                        n = T - jt * P
                        mm = nc.tensor.matmul(ps[:, O, jt * P:T], v_cur[:, jt * P:(jt + 1) * P],
                                              s_T[:, S_AT[jt]:S_AT[jt] + n], start=(jt == 0), stop=(jt == 3),
                                              skip_group_check=True)
                    mm.then_inc(o_ps, 1)
                    pe.wait_ge(evac_dve, ed + h * 2 + 1)
                    unit(uh + 2, 2, 2, h_hi, h_lo)
                    pe.wait_ge(osq_ready, l * HEADS + h + 1)
                    nc.tensor.matmul(ps[:, STAT, :], mean_e[:], buf_a[:, 0, :], start=True, stop=True).then_inc(var_ps, 1)
                    pe.wait_ge(evac_dve, ed + h * 2 + 2)
                    unit(uh + 3, 3, 3, h_hi, h_lo)
                four_units(u0 + U_OUT, xs + XS_Y, y_hi, y_lo, 6)
                for j in range(SLOTS):
                    if j >= 2:
                        pe.wait_ge(evac_dve, ed + (2 + ED_OUT + j - 1))
                    unit(u0 + (U_OUT + SLOTS + j), j, OUT_BANK[j], y_hi, y_lo)
                rms(l * 2 + 1)
                for half in range(2):
                    if half == 0:
                        four_units(u0 + U_UP[0], xs + XS_H2, h_hi, h_lo, 4)
                    with pe.Fori(1 - half, 4) as i:
                        for j in range(SLOTS):
                            pe.wait_ge(evac_act, ea + i * 4 + (EA_UP[half] - 4 + j + 1))
                            if half and j >= 2:
                                pe.wait_ge(evac_dve, ed + (2 + ED_DOWN[0] + 5 + j))
                            unit(u0 + i * SLOTS + (U_UP[half] + j), j, j, h_hi, h_lo)
                    with pe.Fori(0, 4) as i:
                        for m in range(2):
                            pe.wait_ge(evac_act, ea + (EA_UP[half] + 15 + m))
                            pe.wait_ge(evac_dve, ed + i * 2 + (ED_DOWN[half] + m + 1))
                            for kk in range(2):
                                pe.wait_ge(xs_lo, xs + (XS_U[half] + 8 * (kk + 1)))
                                unit(u0 + i * SLOTS + (U_DOWN[half] + 2 * m + kk), 2 * m + kk, 2 + m, u_hi, u_lo,
                                     k0=8 * kk, first=(kk == 0), last=(kk == 1))
                rms(l * 2 + 2)

        @block.scalar
        def _(act):
            def split_hi(l, step, j):
                u = l * UNITS + step * SLOTS + (SLOTS + j)
                act.wait_ge(w_in[j], (l * STEPS + step) * 16 + 32)
                act.wait_ge(pe_unit, u + 1)
                nc.scalar.copy(w_hi[:, j, :], w_raw[:, j, :]).then_inc(w_hi_done, 1)

            def pe_has(l, u):
                act.wait_ge(pe_unit, l * UNITS + u + (SLOTS + 1))

            def norm_root(n):
                act.wait_ge(stat_ps, n + 1)
                nc.scalar.activation(std[:], ps[:, STAT, 0:TOKEN_TILES], ACT.Sqrt, bias=eps[:, 0:1]
                                     ).then_inc(norm_std, 1)

            def norm(n, which):
                for k in range(KT):
                    shift = 2 * k if which == 0 else M_SH2 + k
                    act.wait_ge(xr_ready, n * KT + (k + 1))
                    nc.scalar.activation(h_hi[:, k, :], ring[k % 4], ACT.Identity, bias=mod[:, shift:shift + 1]
                                         ).then_inc(xs_hi, 1)

            def square(n, m, slot, xk):
                act.wait_ge(ssum_added, n * ADDED + m + 1)
                nc.scalar.activation(buf_a[:, slot, :], xk, ACT.Square).then_inc(sq_ready, 1)

            act.sem_inc(std_ready, 1)
            act.wait_ge(c_in, 32)
            nc.scalar.activation(c_col[:, 1, :], c_col[:, 0, :], ACT.Exp, scale=-1.0).then_inc(c_exp, 1)
            for m in range(KT):
                act.wait_ge(x_in[m // 4], 16)
                square(0, m, m % 2, x[:, m, :])
                if m == 2:
                    for i in range(2):
                        act.wait_ge(c_ps, i + 1)
                        nc.scalar.copy(c_act[:, i * T:(i + 1) * T], ps[:, i, :]).then_inc(c_ready, 1)
            act.wait_ge(consts, 1)
            norm_root(0)
            for j in range(SLOTS):
                act.wait_ge(w_in[j], 16)
                nc.scalar.copy(w_hi[:, j, :], w_raw[:, j, :]).then_inc(w_hi_done, 1)
            for k in range(KT):
                act.wait_ge(xr_ready, k + 1)
                if k >= 2:
                    act.wait_ge(xs_lo, k - 1)
                nc.scalar.activation(buf_b[:, k % 2, :], buf_a[:, k % 2, :], ACT.Identity, bias=mod[:, 2 * k:2 * k + 1]
                                     ).then_inc(hf_ready, 1)
                act.wait_ge(hf_ready, k + 1)
                nc.scalar.copy(h_hi[:, k, :], buf_b[:, k % 2, :]).then_inc(xs_hi, 1)

            with act.Fori(0, DEPTH) as l:
                for j in range(SLOTS):
                    pe_has(l, U_V + j)
                    nc.scalar.copy(v_T[:, j, :], ps[:, j, :]).then_inc(evac_act, 1)
                    split_hi(l, 0, j)
                with act.Fori(0, 2) as i:
                    for j in range(SLOTS):
                        pe_has(l, i * 4 + (U_QK + j))
                        act.wait_ge(rope_done, l * 8 + i * 4 + (j + 1))
                        nc.scalar.copy(buf_b[0:64, j % 2, :], ps[64:128, j, :])
                        nc.scalar.copy(buf_b[64:128, j % 2, :], ps[0:64, j, :])
                        nc.scalar.copy(buf_a[:, j % 2, :], ps[:, j, :]).then_inc(evac_act, 1)
                        split_hi(l, i + 1, j)
                with act.Fori(0, HEADS) as h:
                    n = l * HEADS + h
                    pe_has(l, h * 4 + U_HEAD)
                    nc.scalar.activation(egr[:], ps[:, 0, :], ACT.Exp, scale=-1.0)
                    nc.scalar.copy(gr[:], ps[:, 0, :]).then_inc(evac_act, 1)
                    split_hi(l, h + 3, 0)
                    pe_has(l, h * 4 + (U_HEAD + 1))
                    nc.scalar.copy(cc[:], ps[:, 1, :]).then_inc(evac_act, 1)
                    split_hi(l, h + 3, 1)
                    act.wait_ge(rope_done, l * 8 + 10)
                    act.wait_ge(o_ps, n + 2)
                    nc.scalar.activation(buf_a[:, 0, :], ps[:, O, :], ACT.Square).then_inc(osq_ready, 1)
                    split_hi(l, h + 3, 2)
                    act.wait_ge(var_ps, n + 1)
                    nc.scalar.activation(buf_a[:, 1, :], ps[:, STAT, :], ACT.Sqrt, bias=eps[:, 0:1]).then_inc(std_ready, 1)
                    act.wait_ge(evac_dve, l * ED + h * 2 + (ED_HEAD + 4))
                    nc.scalar.copy(y_hi[:, bass.ds(h * 2, 1), :].rearrange("p a t -> p (a t)"), conv[:]).then_inc(xs_hi, 1)
                    act.wait_ge(gate_step, n * 3 + 3)
                    nc.scalar.copy(y_hi[:, bass.ds(h * 2 + 1, 1), :].rearrange("p a t -> p (a t)"), buf_b[:, 1, :]
                                   ).then_inc(xs_hi, 1)
                    split_hi(l, h + 3, 3)
                for i in range(2):
                    for j in range(SLOTS):
                        m = 4 * i + j
                        if m < KT - 1:
                            split_hi(l, 7 + i, j)
                        act.wait_ge(evac_dve, l * ED + (2 + ED_OUT + m + 1))
                        square(l * 2 + 1, m, m % 2, x[:, m, :])
                split_hi(l, 8, 3)
                norm_root(l * 2 + 1)
                norm(l * 2 + 1, 1)
                for half in range(2):
                    with act.Fori(0, 4) as i:
                        for j in range(SLOTS):
                            pe_has(l, i * 4 + (U_UP[half] + j))
                            nc.scalar.activation(buf_a[:, j % 2, :], ps[:, j, :], ACT.Relu).then_inc(evac_act, 1)
                            split_hi(l, i + (9 + 8 * half), j)
                            act.wait_ge(rsq_ready, l * 32 + i * 4 + (16 * half + j + 1))
                            nc.scalar.copy(u_hi[:, bass.ds(i * 4 + j, 1), :].rearrange("p a t -> p (a t)"),
                                           buf_b[:, j % 2, :]).then_inc(xs_hi, 1)
                    if half == 0:
                        with act.Fori(0, 4) as i:
                            for j in range(SLOTS):
                                split_hi(l, i + 13, j)

                def down_square(i, m):
                    act.wait_ge(evac_dve, l * ED + i * 2 + (2 + ED_DOWN[1] + m + 1))
                    square(l * 2 + 2, i * 2 + m, m, x[:, bass.ds(i * 2 + m, 1), :].rearrange("p a t -> p (a t)"))

                with act.Fori(0, 3) as i:
                    for m in range(2):
                        split_hi(l, i + 21, 2 * m)
                        down_square(i, m)
                        split_hi(l, i + 21, 2 * m + 1)
                with act.If(l < DEPTH - 1):
                    split_hi(l, 24, 0)
                down_square(3, 0)
                with act.If(l < DEPTH - 1):
                    split_hi(l, 24, 1)
                    split_hi(l, 24, 2)
                down_square(3, 1)
                with act.If(l < DEPTH - 1):
                    split_hi(l, 24, 3)
                norm_root(l * 2 + 2)
                with act.If(l < DEPTH - 1):
                    norm(l * 2 + 2, 0)

        @block.vector
        def _(dve):
            def split_lo(l, step, j):
                dve.wait_ge(w_hi_done, l * UNITS + step * SLOTS + (SLOTS + j + 1))
                nc.vector.tensor_tensor(w_lo[:, j, :], w_raw[:, j, :], w_hi[:, j, :].bitcast(F32), ALU.subtract
                                        ).then_inc(w_lo_done, 1)

            def pe_has(l, u):
                dve.wait_ge(pe_unit, l * UNITS + u + (SLOTS + 1))

            def reduce_ada(use, slot, j, pair):
                dve.wait_ge(ada_in[slot], use * 16 + 16)
                if j == 0:
                    dve.wait_ge(mod_added, pair + KT)
                nc.vector.tensor_tensor_reduce(out=ada_raw[:, slot, :], in0=ada_raw[:, slot, :], in1=c_act[:],
                                               scale=1.0, scalar=0.0, op0=ALU.mult, op1=ALU.add,
                                               accum_out=ada_sum[:, j:j + 1]).then_inc(ada_done, 1)

            def add_bias(pair, col):
                dve.wait_ge(ada_done, pair * 2 + (SLOTS + 2))
                nc.vector.tensor_tensor(mod[:, bass.ds(col, 2)], ada_sum[:],
                                        bia[:, bass.ds(below(pair * 2 + FIRST_MODS, DEPTH * MODS, 2), 2)],
                                        ALU.add).then_inc(mod_added, 1)

            def early_ada(l, b):
                pair = l * (MODS // 2) + b // 2
                reduce_ada(l * (4 if b % SLOTS >= 2 else 20) + b // SLOTS, b % SLOTS, b % 2, pair)
                if b % 2:
                    add_bias(pair, FIRST_MODS + b - 1)

            def ada_pair(l, p, col, j):
                reduce_ada(l * 20 + p - 4, j, j, l * (MODS // 2) + p)
                if j:
                    add_bias(l * (MODS // 2) + p, col)

            def xs_low(l, i, out, full, hi):
                dve.wait_ge(xs_hi, l * XS + i + 1)
                nc.vector.tensor_tensor(out, full, hi.bitcast(F32), ALU.subtract).then_inc(xs_lo, 1)

            def norm_scale(n):
                dve.wait_ge(norm_std, n + 1)
                nc.vector.reciprocal(rstd[:], std[:]).then_inc(norm_r, 1)
                dve.wait_ge(norm_r, n * 2 + 1)
                nc.vector.tensor_tensor(ssum[:].rearrange("p (a b) -> p a b", b=P),
                                        ident[:].unsqueeze(1).to_broadcast([P, TOKEN_TILES, P]),
                                        rstd[:].unsqueeze(2).to_broadcast([P, TOKEN_TILES, P]), ALU.mult
                                        ).then_inc(norm_r, 1)

            def norm_gain(n, which, scale, g):
                nc.vector.scalar_tensor_tensor(out=gm[:, which, :], in0=scale, scalar=1.0, in1=g,
                                               op0=ALU.add, op1=ALU.mult).then_inc(gm_ready, 1)

            def norm(l, n, which, xs0):
                dve.wait_ge(gm_ready, n + (KT - 1) + 1)
                dve.wait_ge(rinv_ps, n + 1)
                for k in range(KT + 1):
                    if k < KT:
                        if k >= 4:
                            dve.wait_ge(xs_lo, l * XS + (xs0 + k - 3))
                        nc.vector.scalar_tensor_tensor(out=ring[k % 4], in0=x[:, k, :], scalar=gm[:, which, k:k + 1],
                                                       in1=rinv, op0=ALU.mult, op1=ALU.mult).then_inc(xr_ready, 1)
                    if k >= 1:
                        shift = 2 * (k - 1) if which == 0 else M_SH2 + k - 1
                        dve.wait_ge(xs_hi, l * XS + (xs0 + k))
                        nc.vector.scalar_tensor_tensor(out=h_lo[:, k - 1, :], in0=ring[(k - 1) % 4],
                                                       scalar=mod[:, shift:shift + 1],
                                                       in1=h_hi[:, k - 1, :].bitcast(F32),
                                                       op0=ALU.add, op1=ALU.subtract).then_inc(xs_lo, 1)

            def center_v(l):
                for h in range(HEADS):
                    dve.wait_ge(v_turned, l * HEADS + (h + 1))
                    dve.wait_ge(v_centered, l * HEADS + (h + 1))
                    vp = ps[:, 4 + h, :].rearrange("p (j e) -> p j e", e=P)
                    nc.vector.tensor_reduce(vsum[:], vp, AX_X, ALU.add).then_inc(v_summed, 1)
                    dve.wait_ge(v_summed, l * HEADS + (h + 1))
                    nc.vector.scalar_tensor_tensor(
                        out=v_tok[:, h, :].rearrange("p (j e) -> p j e", e=P),
                        in0=vsum[:].unsqueeze(2).to_broadcast([P, T // P, P]), scalar=-1.0 / P, in1=vp,
                        op0=ALU.mult, op1=ALU.add).then_inc(v_centered, 1)

            def residual(m, bank, gate_col):
                xm = x[:, bass.ds(m, 1), :].rearrange("p a t -> p (a t)")
                nc.vector.scalar_tensor_tensor(out=xm, in0=ps[:, bank, :], scalar=mod[:, bass.ds(m + gate_col, 1)],
                                               in1=xm, op0=ALU.mult, op1=ALU.add).then_inc(evac_dve, 1)

            dve.sem_inc(w_lo_done, SLOTS)
            dve.sem_inc(ada_done, SLOTS)
            dve.sem_inc(evac_dve, 2)
            for s in (v_centered, o_read, conv_step):
                dve.sem_inc(s, 1)
            nc.vector.memset(eps[:], EPS)
            nc.vector.memset(z[:], 0.0)
            nc.vector.memset(mean_d[:], 1.0 / D)
            nc.vector.memset(ones[:], 1.0)
            nc.vector.memset(mean_e[:], 1.0 / P).then_inc(consts, 1)
            dve.wait_ge(c_exp, 1)
            nc.vector.tensor_scalar(c_col[:, 1, :], c_col[:, 1, :], 1.0, None, ALU.add).then_inc(c_step, 1)
            dve.wait_ge(c_step, 1)
            nc.vector.reciprocal(c_col[:, 1, :], c_col[:, 1, :]).then_inc(c_step, 1)
            dve.wait_ge(c_step, 2)
            nc.vector.tensor_tensor(c_col[:, 1, :], c_col[:, 0, :], c_col[:, 1, :], ALU.mult).then_inc(c_step, 1)
            dve.wait_ge(c_step, 3)
            nc.vector.tensor_tensor(ada_raw[:, 0, :].rearrange("p (a b) -> p a b", b=P),
                                    ident[:].unsqueeze(1).to_broadcast([P, KT, P]),
                                    c_col[:, 1, :].unsqueeze(2).to_broadcast([P, KT, P]), ALU.mult
                                    ).then_inc(c_step, 1)
            dve.wait_ge(c_ready, 2)
            for k in range(KT):
                dve.wait_ge(ada0_in[k], 16)
                if k:
                    dve.wait_ge(mod_added, k)
                for j in range(2):
                    m = 2 * k + j
                    nc.vector.tensor_tensor_reduce(out=arena[:, m, :], in0=arena[:, m, :], in1=c_act[:],
                                                   scale=1.0, scalar=0.0, op0=ALU.mult, op1=ALU.add,
                                                   accum_out=ada_sum[:, j:j + 1]).then_inc(ada0_done, 1)
                if k == 0:
                    norm_scale(0)
                    dve.wait_ge(par_in, 48)
                dve.wait_ge(ada0_done, 2 * k + 2)
                nc.vector.tensor_tensor(mod[:, 2 * k:2 * k + 2], ada_sum[:], bia[:, 2 * k:2 * k + 2], ALU.add
                                        ).then_inc(mod_added, 1)
                dve.wait_ge(mod_added, k + 1)
                nc.vector.scalar_tensor_tensor(out=gm[:, 0, k:k + 1], in0=mod[:, 2 * k + 1:2 * k + 2], scalar=1.0,
                                               in1=par[:, C_G1 + k:C_G1 + k + 1], op0=ALU.add, op1=ALU.mult
                                               ).then_inc(gm_ready, 1)
                dve.wait_ge(gm_ready, k + 1)
                if k == 0:
                    dve.wait_ge(rinv_ps, 1)
                if k >= 2:
                    dve.wait_ge(hf_ready, k - 1)
                nc.vector.scalar_tensor_tensor(out=buf_a[:, k % 2, :], in0=x[:, k, :], scalar=gm[:, 0, k:k + 1],
                                               in1=rinv, op0=ALU.mult, op1=ALU.mult).then_inc(xr_ready, 1)
                if k == 0:
                    for j in range(SLOTS):
                        dve.wait_ge(w_hi_done, j + 1)
                        nc.vector.tensor_tensor(w_lo[:, j, :], w_raw[:, j, :], w_hi[:, j, :].bitcast(F32), ALU.subtract
                                                ).then_inc(w_lo_done, 1)
            dve.wait_ge(tab_in, 16)

            with dve.Fori(0, DEPTH) as l:
                for j in range(SLOTS):
                    split_lo(l, 0, j)
                    early_ada(l, j)
                for j in range(SLOTS):
                    split_lo(l, 1, j)
                    if j == 1:
                        center_v(l)
                    early_ada(l, 4 + j)
                for j in range(SLOTS):
                    split_lo(l, 2, j)
                    early_ada(l, 8 + 2 * j)
                    early_ada(l, 9 + 2 * j)
                with dve.Fori(0, HEADS) as h:
                    n = l * HEADS + h

                    split_lo(l, h + 3, 0)
                    for jt in range(TOKEN_TILES):
                        if jt != 3:
                            dve.wait_ge(s_ps, n * 3 + (jt + 1))
                        w = T - jt * P
                        nc.vector.tensor_tensor(s_T[:, S_AT[jt]:S_AT[jt] + w],
                                                ps[:, S_BANK[jt], S_COL[jt]:S_COL[jt] + w],
                                                decay[:, bass.ds(h, 1), 0:w].rearrange("p a t -> p (a t)"), ALU.mult
                                                ).then_inc(s_ready, 1)
                    ada_pair(l, h + 8, h * 2 + (FIRST_MODS + 16), 0)
                    split_lo(l, h + 3, 1)
                    ada_pair(l, h + 8, h * 2 + (FIRST_MODS + 16), 1)
                    pe_has(l, h * 4 + (U_HEAD + 2))
                    dve.wait_ge(evac_act, l * EA + h * 2 + (EA_HEAD + 2))
                    dve.wait_ge(conv_step, n * 3 + 1)
                    nc.vector.tensor_tensor(z[:, 2:T + 2], ps[:, 2, :], cc, ALU.mult).then_inc(evac_dve, 1)
                    split_lo(l, h + 3, 2)
                    tap = [par[:, bass.ds(l * PARAMS + h * 3 + (C_CONV + t), 1)] for t in range(3)]
                    dve.wait_ge(evac_dve, l * ED + h * 2 + (2 + ED_HEAD + 1))
                    dve.wait_ge(xs_lo, l * XS + h * 2 + XS_Y)
                    nc.vector.tensor_scalar(conv, z[:, 0:T], tap[0], None, ALU.mult).then_inc(conv_step, 1)
                    for t in (1, 2):
                        dve.wait_ge(conv_step, n * 3 + (t + 1))
                        nc.vector.scalar_tensor_tensor(out=conv, in0=z[:, t:t + T], scalar=tap[t], in1=conv,
                                                       op0=ALU.mult, op1=ALU.add).then_inc(conv_step, 1)
                    dve.wait_ge(var_ps, n + 1)
                    nc.vector.scalar_tensor_tensor(out=buf_b[:, 1, :], in0=ps[:, O, :],
                                                   scalar=par[:, bass.ds(l * PARAMS + h + C_RET, 1)], in1=gr[:],
                                                   op0=ALU.mult, op1=ALU.mult).then_inc(o_read, 1)
                    dve.wait_ge(std_ready, n + 2)
                    nc.vector.scalar_tensor_tensor(out=egr[:], in0=egr[:], scalar=1.0, in1=buf_a[:, 1, :],
                                                   op0=ALU.add, op1=ALU.mult).then_inc(gate_step, 1)
                    dve.wait_ge(gate_step, n * 3 + 1)
                    nc.vector.reciprocal(buf_b[:, 0, :], egr[:]).then_inc(gate_step, 1)
                    pe_has(l, h * 4 + (U_HEAD + 3))
                    dve.wait_ge(conv_step, n * 3 + 4)
                    nc.vector.tensor_tensor(conv, ps[:, 3, :], conv, ALU.mult).then_inc(evac_dve, 1)
                    dve.wait_ge(gate_step, n * 3 + 2)
                    nc.vector.tensor_tensor(buf_b[:, 1, :], buf_b[:, 1, :], buf_b[:, 0, :], ALU.mult
                                            ).then_inc(gate_step, 1)
                    xs_low(l, h * 2 + XS_Y, y_lo[:, bass.ds(h * 2, 1), :].rearrange("p a t -> p (a t)"), conv,
                           y_hi[:, bass.ds(h * 2, 1), :].rearrange("p a t -> p (a t)"))
                    xs_low(l, h * 2 + (XS_Y + 1), y_lo[:, bass.ds(h * 2 + 1, 1), :].rearrange("p a t -> p (a t)"),
                           buf_b[:, 1, :], y_hi[:, bass.ds(h * 2 + 1, 1), :].rearrange("p a t -> p (a t)"))
                    split_lo(l, h + 3, 3)
                dve.wait_ge(mod_added, l * 24 + 20)
                norm_gain(l * 2 + 1, 1, mod[:, M_SC2:M_SC2 + KT], par[:, bass.ds(l * PARAMS + C_G2, KT)])
                for i in range(2):
                    for j in range(SLOTS):
                        m = 4 * i + j
                        if i == 0:
                            split_lo(l, 7, j)
                        pe_has(l, U_OUT + m)
                        residual(m, OUT_BANK[j] if i else j, M_GATE1)
                        if i == 1:
                            split_lo(l, 8, j)
                norm_scale(l * 2 + 1)
                norm(l, l * 2 + 1, 1, XS_H2)
                for half in range(2):
                    with dve.Fori(0, 4) as i:
                        for j in range(SLOTS):
                            split_lo(l, i + (9 + 8 * half), j)
                            ub = bass.ds(i * 4 + j, 1)
                            xs_low(l, i * 4 + (XS_U[half] + j), u_lo[:, ub, :].rearrange("p a t -> p (a t)"),
                                   buf_b[:, j % 2, :], u_hi[:, ub, :].rearrange("p a t -> p (a t)"))
                            if half == 0 and j < 2:
                                ada_pair(l, i + 12, i * 2 + M_GATE2, j)
                        if half:
                            with dve.If(l < DEPTH - 1):
                                for j in range(2):
                                    ada_pair(l, i + 20, i * 2 + KT, j)
                    if half == 0:
                        with dve.Fori(0, 4) as i:
                            for m in range(2):
                                split_lo(l, i + 13, 2 * m)
                                pe_has(l, i * 4 + (U_DOWN[0] + 2 * m + 1))
                                dve.wait_ge(mod_added, l * 24 + 24)
                                residual(i * 2 + m, 2 + m, M_GATE2)
                                split_lo(l, i + 13, 2 * m + 1)
                            with dve.If(l < DEPTH - 1):
                                for j in range(2):
                                    ada_pair(l, i + 16, i * 2, j)
                    else:
                        with dve.Fori(0, 3) as i:
                            for m in range(2):
                                split_lo(l, i + 21, 2 * m)
                                pe_has(l, i * 4 + (U_DOWN[1] + 2 * m + 1))
                                residual(i * 2 + m, 2 + m, M_GATE2)
                                split_lo(l, i + 21, 2 * m + 1)
                        with dve.If(l < DEPTH - 1):
                            dve.wait_ge(mod_added, l * 24 + 32)
                            norm_gain(l * 2 + 2, 0, mod[:, 1:2 * KT:2], par[:, bass.ds(below(l * PARAMS + PARAMS + C_G1, DEPTH * PARAMS, KT), KT)])
                            split_lo(l, 24, 0)
                        pe_has(l, U_DOWN[1] + 13)
                        residual(6, 2, M_GATE2)
                        with dve.If(l < DEPTH - 1):
                            split_lo(l, 24, 1)
                            split_lo(l, 24, 2)
                        pe_has(l, U_DOWN[1] + 15)
                        residual(7, 3, M_GATE2)
                        with dve.If(l < DEPTH - 1):
                            split_lo(l, 24, 3)
                norm_scale(l * 2 + 2)
                with dve.If(l < DEPTH - 1):
                    norm(l + 1, l * 2 + 2, 0, XS_H)
            dve.wait_ge(rinv_ps, 2 * DEPTH + 1)
            for k in range(KT):
                nc.vector.scalar_tensor_tensor(out=x[:, k, :], in0=x[:, k, :], scalar=fin_g[:, k:k + 1], in1=rinv,
                                               op0=ALU.mult, op1=ALU.mult).then_inc(out_ready, 1)

        @block.gpsimd
        def _(pool):
            def clear_sum(n):
                if not (isinstance(n, int) and n == 0):
                    pool.wait_ge(rinv_ps, n)
                else:
                    pool.wait_ge(consts, 1)
                zero = z[:, 0:1].to_broadcast([P, T])
                nc.gpsimd.tensor_tensor(ssum[:], zero, zero, ALU.add).then_inc(ssum_clear, 1)

            def add_square(n, m, slot):
                pool.wait_ge(sq_ready, n * KT + m + 1)
                pool.wait_ge(ssum_clear, n + 1)
                pool.wait_ge(ssum_added, n * ADDED + m + 2)
                nc.gpsimd.tensor_tensor(ssum[:], ssum[:], buf_a[:, slot, :], ALU.add).then_inc(ssum_added, 1)

            pool.sem_inc(ssum_added, 2)
            pool.sem_inc(rope_done, 2)
            clear_sum(0)
            for m in range(ADDED):
                add_square(0, m, m % 2)
            for k in range(KT):
                pool.wait_ge(xs_hi, k + 1)
                nc.gpsimd.tensor_tensor(h_lo[:, k, :], buf_b[:, k % 2, :], h_hi[:, k, :].bitcast(F32), ALU.subtract
                                        ).then_inc(xs_lo, 1)
            pool.wait_ge(tab_in, 16)
            with pool.Fori(0, DEPTH) as l:
                def current(h, n, roped):
                    zero = z[:, 0:1].to_broadcast([P, T])
                    pool.wait_ge(rope_done, l * 8 + roped)
                    pool.wait_ge(o_ps, n + 1)
                    nc.gpsimd.tensor_tensor(k_cur[:], qkT[:, bass.ds(h * 2 + 1, 1), :].rearrange("p a t -> p (a t)"),
                                            zero, ALU.add)
                    pool.wait_ge(v_centered, n + 2)
                    nc.gpsimd.tensor_tensor(v_cur[:], v_tok[:, bass.ds(h, 1), :].rearrange("p a t -> p (a t)"),
                                            zero, ALU.add).then_inc(cur_ready, 1)

                for j in range(2 * SLOTS):
                    a, b = buf_a[:, j % 2, :], buf_b[:, j % 2, :]
                    pool.wait_ge(evac_act, l * EA + (EA_QK + j + 1))
                    nc.gpsimd.tensor_tensor(a, a, cos, ALU.mult)
                    nc.gpsimd.tensor_tensor(b, b, sin, ALU.mult).then_inc(rope_step, 1)
                    pool.wait_ge(rope_step, l * 8 + (j + 1))
                    nc.gpsimd.tensor_tensor(qkT[:, j, :], a, b, ALU.add).then_inc(rope_done, 1)
                    if j == 5:
                        current(0, l * HEADS, 4)
                with pool.Fori(1, HEADS) as h:
                    current(h, l * HEADS + h, 10)
                clear_sum(l * 2 + 1)
                for m in range(ADDED):
                    add_square(l * 2 + 1, m, m % 2)
                for half in range(2):
                    with pool.Fori(0, 4) as i:
                        for j in range(SLOTS):
                            pool.wait_ge(evac_act, l * EA + i * 4 + (EA_UP[half] + j + 1))
                            pool.wait_ge(xs_lo, l * XS + i * 4 + (XS_U[half] + j - 1))
                            nc.gpsimd.tensor_tensor(buf_b[:, j % 2, :], buf_a[:, j % 2, :], buf_a[:, j % 2, :], ALU.mult
                                                    ).then_inc(rsq_ready, 1)
                clear_sum(l * 2 + 2)
                with pool.Fori(0, 3) as i:
                    for m in range(2):
                        add_square(l * 2 + 2, i * 2 + m, m)
                add_square(l * 2 + 2, 6, 0)


def shape_tables():
    import numpy as np
    decay = np.zeros((HEADS, P, T), np.float64)
    off = np.arange(T)[None, :] - np.arange(P)[:, None]
    for h in range(HEADS):
        log_g = np.log1p(-np.exp2(-5.0 - h))
        decay[h] = np.where(off >= 0, np.exp(log_g * np.maximum(off, 0)), 0.0) * P ** -0.5
    half = P // 2
    inv = np.float32(10000.0) ** (-np.arange(0, P, 2, dtype=np.float32) / np.float32(P))
    ang = inv[:, None] * np.arange(T, dtype=np.float32)[None, :]
    cos = np.concatenate([np.cos(ang), np.cos(ang)])
    sin = np.concatenate([-np.sin(ang), np.sin(ang)])
    assert cos.shape == (2 * half, T)
    parts = [decay.transpose(1, 0, 2).reshape(P, HEADS * T), cos, sin]
    return np.ascontiguousarray(np.concatenate([p.astype(np.float32) for p in parts], axis=1))


def columns(w):
    k, n = w.shape
    return w.reshape(k // P, P, n // P, P).transpose(2, 0, 1, 3)


def weight_stream(w_in, w_out, w_up, w_down):
    import numpy as np
    units = []
    for l in range(DEPTH):
        t = columns(w_in[l])
        cb, ccs, cu, q, k, v, g = (t[4 * i:4 * i + 4] for i in range(7))
        units += list(v)
        for h in range(HEADS):
            units += [q[h], k[h]]
        for h in range(HEADS):
            units += [g[h], ccs[h], cu[h], cb[h]]
        order = [half * HEADS + h for h in range(HEADS) for half in range(2)]
        units += list(columns(w_out[l])[:, order])
        up, down = columns(w_up[l]), columns(w_down[l])
        for half in range(2):
            units += list(up[half * HALF_TILES:(half + 1) * HALF_TILES])
            for m in range(KT):
                for kk in range(2):
                    k0 = half * HALF_TILES + 8 * kk
                    units.append(down[m, k0:k0 + 8])
    out = np.empty((len(units), P, KT, P), np.float32)
    for i, u in enumerate(units):
        out[i] = u.transpose(1, 0, 2)
    return out.reshape(len(units), P, D)


def kernel(x, c, norm1_g, w_in, conv_w, ret_norm_g, w_out, norm2_g, w_up, w_down, w_ada, b_ada, final_g):
    import numpy as np
    import concourse.bacc as bacc
    from concourse.bass_utils import run_bass_kernel_spmd

    cols = lambda a: np.asarray(a).reshape(-1, P).T
    params = []
    for l in range(DEPTH):
        params += [cols(norm1_g[l]), cols(norm2_g[l]),
                   np.asarray(conv_w[l]).reshape(3, HEADS, P).transpose(2, 1, 0).reshape(P, 12), cols(ret_norm_g[l])]
    mods = [half * KT + k for k in range(KT) for half in range(2)] + list(range(2 * KT, MODS))
    mods = [l * MODS + m for l in range(DEPTH) for m in mods]
    arrays = {
        "xT": np.asarray(x)[0].T.reshape(KT, P, T),
        "c_cols": cols(c),
        "weights": weight_stream(*(np.asarray(w) for w in (w_in, w_out, w_up, w_down))),
        "ada": np.asarray(w_ada).transpose(0, 2, 1).reshape(DEPTH * MODS, P, D)[mods],
        "params": np.concatenate(params, axis=1),
        "bias": cols(b_ada)[:, mods],
        "final_g": cols(final_g),
        "identity": np.eye(P, dtype=np.float32),
        "tables": shape_tables(),
    }
    arrays = {k: np.ascontiguousarray(v) for k, v in arrays.items()}
    nc = bacc.Bacc("TRN2", target_bir_lowering=False, num_devices=1)
    aps = {k: nc.dram_tensor(k, v.shape, mybir.dt.from_np(v.dtype), kind="ExternalInput").ap()
           for k, v in arrays.items()}
    outT = nc.dram_tensor("outT", (KT, P, T), F32, kind="ExternalOutput").ap()
    trunk(nc, **aps, outT=outT)
    result = run_bass_kernel_spmd(nc, [arrays], core_ids=[0])
    return np.ascontiguousarray(result.results[0]["outT"].reshape(D, T).T).reshape(1, T, D)
```

```python
from contextlib import ExitStack

import concourse.bass as bass
from concourse import mybir

P = 128
D = 1024
T = 512
DEPTH = 2
KT = D // P
HEADS = 4
EPS = 1e-6
SLOTS = 4
UNITS = 100
STEPS = UNITS // SLOTS
MODS = 6 * KT
TOKEN_TILES = T // P
HALVES = (slice(0, T // 2), slice(T // 2, T))
WHOLE = slice(0, T)
HALVES_D = (slice(0, D // 2), slice(D // 2, D))
SQ_MIX, SQ_MLP = 4 + 2 * 4, 6 + 2 * 2
SQ = SQ_MIX + SQ_MLP
FIRST_MODS = 2 * KT
HALF_TILES = 16

U_V, U_QK, U_HEAD, U_OUT = 0, 4, 12, 28
U_UP = (36, 68)
U_DOWN = (52, 84)
EA_QK, EA_HEAD, EA_UP = 0, 8, (16, 32)
EA = 48
ED_HEAD, ED_OUT, ED_DOWN = 0, 8, (20, 28)
ED = 38
XS_H, XS_Y, XS_H2, XS_U = 0, 16, 24, (40, 56)
XS = 72
C_G1, C_G2, C_CONV, C_RET = 0, 8, 16, 28
PARAMS = 32
M_GATE1, M_SH2, M_SC2, M_GATE2 = range(2 * KT, MODS, KT)

F32 = mybir.dt.float32
F32R = mybir.dt.float32r
ALU = mybir.AluOpType
ACT = mybir.ActivationFunctionType
AX_X = mybir.AxisListType.X


def trunk(nc, xT, c_cols, weights, ada, params, bias, final_g, identity, tables, outT):
    with ExitStack() as ctx:
        def sb(name, shape, dt=F32):
            return ctx.enter_context(nc.sbuf_tensor(name, shape, dt))

        def sem(name):
            return ctx.enter_context(nc.semaphore(name))

        arena_at = -(-nc.sbuf_base // 32) * 32
        arena = sb("arena", [P, 16, D])
        over = [arena_at]

        def view(name, shape, dt=F32):
            size = 4
            for n in shape[1:]:
                size *= n
            t = nc.alloc_sbuf_tensor_at(name, shape, dt, offset=over[0])
            over[0] += size
            assert over[0] <= arena_at + 16 * D * 4
            return t

        u_hi = view("u_hi", [P, HALF_TILES, T], F32R)
        u_lo = view("u_lo", [P, HALF_TILES, T], F32R)
        over[0] = arena_at
        y_hi = view("y_hi", [P, KT, T], F32R)
        qk_at = over[0]
        qkT = view("qkT", [P, 2 * HEADS, T])
        v_tok = view("v_tok", [P, HEADS, T])
        conv = view("conv", [P, T])[:]
        cc = view("cc", [P, T])[:]
        k_hi = view("k_hi", [P, T], F32R)
        k_lo = view("k_lo", [P, T], F32R)
        k_last = view("k_last", [P, P])
        v_cur = view("v_cur", [P, T])
        s_T = view("s_T", [P, 1280])
        gr = view("gr", [P, T])
        egr = view("egr", [P, T])
        q_hi = view("q_hi", [P, T], F32R)
        q_lo = view("q_lo", [P, T], F32R)
        osq_hi, osq_lo = q_hi, q_lo
        over[0] = qk_at
        y_lo = view("y_lo", [P, KT, T], F32R)

        x = sb("x", [P, KT, T])
        h_hi = sb("h_hi", [P, KT, T], F32R)
        h_lo = sb("h_lo", [P, KT, T], F32R)
        w_raw = sb("w_raw", [P, SLOTS, D])
        w_hi = sb("w_hi", [P, SLOTS, D], F32R)
        w_lo = sb("w_lo", [P, SLOTS, D], F32R)
        ada_raw = sb("ada_raw", [P, SLOTS, D])
        tab = sb("tab", [P, tables.shape[1]])
        decay = tab[:, 0:HEADS * T].rearrange("p (h t) -> p h t", h=HEADS)
        cos = tab[:, HEADS * T:HEADS * T + T]
        sin = tab[:, HEADS * T + T:HEADS * T + 2 * T]
        ident = sb("ident", [P, P])
        c_col = sb("c_col", [P, 2, KT])
        c_act = sb("c_act", [P, D])
        par = sb("par", [P, DEPTH * PARAMS])
        bia = sb("bia", [P, DEPTH * MODS])
        fin_g = sb("fin_g", [P, KT])
        mod = sb("mod", [P, MODS])
        ada_sum = sb("ada_sum", [P, 2])
        sh_sum = sb("sh_sum", [P, KT])
        sc_sum = sb("sc_sum", [P, KT])
        sc_bias = sb("sc_bias", [P, KT])
        warm = sb("warm", [P, 1])
        gm = sb("gm", [P, 2, KT])
        eps = sb("eps", [P, 1])
        vsum = sb("vsum", [P, HEADS])
        ones = sb("ones", [P, P])
        mean_d = sb("mean_d", [P, 1])
        mean_e = sb("mean_e", [P, P], F32R)
        buf_a = sb("buf_a", [P, 2, T])
        buf_b = sb("buf_b", [P, 2, T])
        ring = [buf_a[:, 0, :], buf_a[:, 1, :], buf_b[:, 0, :], buf_b[:, 1, :]]
        ssum = sb("ssum", [P, T])
        std = sb("std", [P, TOKEN_TILES])
        rstd = sb("rstd", [P, TOKEN_TILES])
        z = sb("z", [P, T + 2])

        ps = ctx.enter_context(nc.psum_tensor("ps", [P, 8, T], F32))
        S_BANK = (4, 5, 6, 6)
        S_COL = (0, 0, 0, 256)
        S_AT = (0, 512, 896, 1152)
        STAT, RMS, O = 4, 5, 7
        OUT_BANK = ((6, 7, 0, 1), (2, 3, 6, 7))
        QK_BANK = (6, 7, 2, 3)
        DOWN_BANK = ((2, 3), (6, 7))
        rinv = ps[:, RMS, :]

        c_in, par_in, rope_in, decay_in = sem("c_in"), sem("par_in"), sem("rope_in"), sem("decay_in")
        x_in = [sem(f"x_in{i}") for i in range(2)]
        sh_in = [sem(f"sh_in{i}") for i in range(KT)]
        sc_in = [sem(f"sc_in{i}") for i in range(KT)]
        w_in = [sem(f"w_in{i}") for i in range(SLOTS)]
        ada_in = [sem(f"ada_in{i}") for i in range(SLOTS)]
        consts = sem("consts")
        c_exp, c_step, c_ps, c_ready = sem("c_exp"), sem("c_step"), sem("c_ps"), sem("c_ready")
        w_hi_done = sem("w_hi_done")
        w_lo_done = sem("w_lo_done")
        pe_half = sem("pe_half")
        pe_unit = sem("pe_unit")
        ada_done = sem("ada_done")
        x_squared, x_added = sem("x_squared"), sem("x_added")
        sh_product, sh_summed, sh_ready = sem("sh_product"), sem("sh_summed"), sem("sh_ready")
        sc_summed = sem("sc_summed")
        mod_added = sem("mod_added")
        evac_act = sem("evac_act")
        evac_dve = sem("evac_dve")
        xs_hi, xs_lo = sem("xs_hi"), sem("xs_lo")
        sq_ready = sem("sq_ready")
        ssum_added = sem("ssum_added")
        ssum_clear = sem("ssum_clear")
        stat_ps, norm_std, norm_r, rinv_ps = sem("stat_ps"), sem("norm_std"), sem("norm_r"), sem("rinv_ps")
        gm_ready = sem("gm_ready")
        xr_ready = sem("xr_ready")
        rope_step = sem("rope_step")
        rope_done = sem("rope_done")
        v_ready, v_summed = sem("v_ready"), sem("v_summed")
        v_centered = sem("v_centered")
        cur_ready, s_ps, s_ready = sem("cur_ready"), sem("s_ps"), sem("s_ready")
        qk_hi_done, qk_split = sem("qk_hi_done"), sem("qk_split")
        o_ps, o_read, std_ready = sem("o_ps"), sem("o_read"), sem("std_ready")
        osq_ready, osq_hi_done, osq_split = sem("osq_ready"), sem("osq_hi_done"), sem("osq_split")
        var_ps, mean_ready = sem("var_ps"), sem("mean_ready")
        conv_step = sem("conv_step")
        gate_step = sem("gate_step")
        rsq_ready = sem("rsq_ready")
        out_ready, out_done = sem("out_ready"), sem("out_done")

        block = ctx.enter_context(nc.Block())

        def below(value, limit, size=1):
            return nc.s_assert_within(value, 0, limit - size,
                                      skip_runtime_bounds_check_because="under If(l < DEPTH - 1) or If(h < HEADS - 1)")

        @block.sync
        def _(sp):
            def load_weight(l, step, j):
                u = l * UNITS + step * SLOTS + (SLOTS + j)
                sp.wait_ge(w_lo_done, u + 1)
                sp.dma_start(w_raw[:, j, :], weights[bass.ds(below(u, DEPTH * UNITS), 1), :, :].rearrange("a p n -> p (a n)")
                             ).then_inc(w_in[j], 16)

            def load_ada(b, slot, since):
                sp.wait_ge(ada_done, b + (SLOTS - since + 1))
                sp.dma_start(ada_raw[:, slot, :],
                             ada[bass.ds(below(b + FIRST_MODS, DEPTH * MODS), 1), :, :].rearrange("a p n -> p (a n)")
                             ).then_inc(ada_in[slot], 16)

            def load_step(l, step, adas, b, since=SLOTS):
                for j in range(SLOTS):
                    load_weight(l, step, j)
                    for a in range(j * adas // SLOTS, (j + 1) * adas // SLOTS):
                        load_ada(b + a, a % since, since)

            sp.dma_start(c_col[:, 0, :], c_cols).then_inc(c_in, 16)
            sp.dma_start(ident[:], identity).then_inc(c_in, 16)
            for i in range(2):
                sp.dma_start(x[:, 4 * i:4 * i + 4, :], xT[4 * i:4 * i + 4, :, :].rearrange("k p t -> p k t")
                             ).then_inc(x_in[i], 16)
            for i in range(KT):
                sp.dma_start(arena[:, 2 * i, :], ada[2 * i, :, :]).then_inc(sh_in[i], 16)
                sp.dma_start(arena[:, 2 * i + 1, :], ada[2 * i + 1, :, :]).then_inc(sc_in[i], 16)
                if i == 0:
                    sp.dma_start(par[:], params).then_inc(par_in, 16)
                    sp.dma_start(bia[:], bias).then_inc(par_in, 16)
                    sp.dma_start(fin_g[:], final_g).then_inc(par_in, 16)
                    for j in range(SLOTS):
                        sp.dma_start(w_raw[:, j, :], weights[j, :, :]).then_inc(w_in[j], 16)

            with sp.Fori(0, DEPTH) as l:
                b0 = l * MODS
                for j in range(SLOTS):
                    load_weight(l, 0, j)
                with sp.If(l < 1):
                    at = slice(HEADS * T, HEADS * T + 2 * T)
                    sp.dma_start(tab[:, at], tables[:, at]).then_inc(rope_in, 16)
                for j in range(SLOTS):
                    load_ada(b0 + j, j, SLOTS)
                with sp.If(l < 1):
                    at = slice(0, HEADS * T)
                    sp.dma_start(tab[:, at], tables[:, at]).then_inc(decay_in, 16)
                load_step(l, 1, 4, b0 + 4)
                load_step(l, 2, 4, b0 + 8)
                with sp.Fori(0, HEADS) as i:
                    load_step(l, i + 3, 2, b0 + i * 2 + 12, since=2)
                for j in range(SLOTS):
                    load_weight(l, 7, j)
                    load_ada(b0 + (20 + j), j, 2 if j < 2 else SLOTS)
                load_step(l, 8, 0, 0)
                with sp.Fori(0, 4) as i:
                    load_step(l, i + 9, 2, b0 + i * 2 + 24, since=2)
                with sp.Fori(0, 8) as i:
                    load_weight(l, i + 13, 0)
                    load_weight(l, i + 13, 1)
                    with sp.If(l < DEPTH - 1):
                        for a in range(2):
                            load_ada(b0 + i * 2 + (32 + a), a, 2)
                    load_weight(l, i + 13, 2)
                    load_weight(l, i + 13, 3)
                with sp.Fori(0, 3) as i:
                    load_step(l, i + 21, 0, 0)
                with sp.If(l < DEPTH - 1):
                    load_step(l, 24, 0, 0)

            for half, at in enumerate(HALVES):
                for k in range(0, KT, 2):
                    sp.wait_ge(out_ready, half * KT + k + 2)
                    sp.dma_start(outT[k:k + 2, :, at].rearrange("k p t -> p k t"), x[:, k:k + 2, at]
                                 ).then_inc(out_done, 16)
            sp.wait_ge(out_done, 16 * KT)

        @block.tensor
        def _(pe):
            def three(bank, j, k, hi, lo, first, last, at=WHOLE):
                out, hi, lo = ps[:, bank, at], hi[:, at], lo[:, at]
                wh, wl = w_hi[:, j, k * P:(k + 1) * P], w_lo[:, j, k * P:(k + 1) * P]
                nc.tensor.matmul(out, wh, hi, start=first, stop=False, skip_group_check=True)
                nc.tensor.matmul(out, wh, lo, start=False, stop=False, skip_group_check=True)
                return nc.tensor.matmul(out, wl, hi, start=False, stop=last, skip_group_check=True)

            def unit(u, j, bank, hi, lo, k0=0, first=True, last=True):
                pe.wait_ge(w_lo_done, u + (SLOTS + 1))
                for k in range(KT):
                    mm = three(bank, j, k, hi[:, k0 + k, :], lo[:, k0 + k, :], first and k == 0, last and k == KT - 1)
                mm.then_inc(pe_unit, 1)

            def unit_half(j, bank, half, hi, lo, k0=0, first=True, last=True):
                for k in range(KT):
                    mm = three(bank, j, k, hi[:, k0 + k, :], lo[:, k0 + k, :], first and k == 0, last and k == KT - 1,
                               HALVES[half])
                if half:
                    mm.then_inc(pe_unit, 1)
                elif last:
                    mm.then_inc(pe_half, 1)

            def mean_squares(n, half, added, tiles=2):
                pe.wait_ge(ssum_added, added + 2)
                for t in range(half * 2, half * 2 + tiles):
                    mm = nc.tensor.matmul(ps[:, STAT, t:t + 1], ssum[:, t * P:(t + 1) * P], mean_d[:],
                                          start=True, stop=True, skip_group_check=True)
                mm.then_inc(stat_ps, 1)

            def spread(n, half, at):
                pe.wait_ge(norm_r, n * 4 + half * 2)
                nc.tensor.matmul(ps[:, RMS, at], ones[:], ssum[:, at], start=True, stop=True).then_inc(rinv_ps, 1)

            def v_tile(k, t, units, start, last):
                a, b = units
                out = ps[:, t, a * P:b * P].rearrange("p (a n) -> p a n", n=P)
                hh, hl = h_hi[:, k, t * P:(t + 1) * P], h_lo[:, k, t * P:(t + 1) * P]
                wh, wl = w_hi[:, a:b, k * P:(k + 1) * P], w_lo[:, a:b, k * P:(k + 1) * P]
                nc.tensor.matmul(out, hh, wh, start=start, stop=False, skip_group_check=True)
                nc.tensor.matmul(out, hh, wl, start=False, stop=False, skip_group_check=True)
                return nc.tensor.matmul(out, hl, wh, start=False, stop=last, skip_group_check=True)

            def v_end(k0, tiles, xs=None):
                for units in ((0, 2), (2, 4)):
                    for k in range(k0, KT):
                        if xs is not None and units[0] == 0:
                            pe.wait_ge(xs_lo, xs + (k + 1))
                        for t in tiles:
                            mm = v_tile(k, t, units, False, k == KT - 1)
                            if k == KT - 1 and t < 3 and units[0]:
                                mm.then_inc(v_ready, 1)
                    mm.then_inc(pe_unit, 2)

            def v_step(u, xs, n, added):
                for units in ((0, 2), (2, 4)):
                    for j in range(*units):
                        pe.wait_ge(w_lo_done, u + (j + SLOTS + 1))
                    for part in ([0, 1],) if units[0] == 0 else ([0], [1]):
                        for k in range(KT):
                            if units[0] == 0:
                                pe.wait_ge(xs_lo, xs + (k + 1))
                            for t in part:
                                mm = v_tile(k, t, units, units[0] == 0 and k == 0, k == KT - 1)
                        if units[0]:
                            mm.then_inc(v_ready, 1)
                        if part == [0, 1]:
                            mean_squares(n, 1, added)
                        if part == [0]:
                            pe.wait_ge(xr_ready, n * 16)
                            spread(n, 1, HALVES[1])
                for k in range(4):
                    pe.wait_ge(xs_lo, xs + (KT + k + 1))
                    for t in (2, 3):
                        v_tile(k, t, (0, SLOTS), k == 0, False)
                v_end(4, (2, 3), xs + KT)

            def first_step(u, xs, n, added):
                def product(half, j, k):
                    return three(j, j, k, h_hi[:, k, :], h_lo[:, k, :], half == 0 and k == 0, k == KT - 1, HALVES[half])

                for j in range(2):
                    pe.wait_ge(w_lo_done, u + (j + SLOTS + 1))
                    for k in range(4):
                        if j == 0:
                            pe.wait_ge(xs_lo, xs + (k + 1))
                        product(0, j, k)
                for k in range(4, KT):
                    pe.wait_ge(xs_lo, xs + (k + 1))
                    for j in range(2):
                        product(0, j, k)
                mean_squares(n, 1, added)
                for j in (2, 3):
                    pe.wait_ge(w_lo_done, u + (j + SLOTS + 1))
                    for k in range(KT):
                        product(0, j, k)
                    if j == 2:
                        pe.wait_ge(xr_ready, n * 16)
                        spread(n, 1, HALVES[1])
                for k in range(4):
                    pe.wait_ge(xs_lo, xs + (KT + k + 1))
                    for j in range(SLOTS):
                        product(1, j, k)
                for j in range(SLOTS):
                    for k in range(4, KT):
                        if j == 0:
                            pe.wait_ge(xs_lo, xs + (KT + k + 1))
                        mm = product(1, j, k)
                    mm.then_inc(pe_unit, 1)

            pe.sem_inc(pe_unit, SLOTS)
            pe.sem_inc(o_ps, 1)
            pe.wait_ge(consts, 1)
            for i in range(2):
                pe.wait_ge(c_step, 4 + i)
                nc.tensor.matmul(ps[:, i, :], ones[:], ada_raw[:, 0, i * T:(i + 1) * T], start=True, stop=True
                                 ).then_inc(c_ps, 1)
            pe.wait_ge(x_added, KT - 1)
            mean_squares(0, 0, 0, TOKEN_TILES)
            spread(0, 1, WHOLE)
            pe.wait_ge(c_ready, 2)
            pe.wait_ge(mean_ready, 1)
            for k in range(KT):
                pe.wait_ge(xs_lo, 2 * k + 2)
                if k == 0:
                    for units in ((0, 2), (2, 4)):
                        for j in range(*units):
                            pe.wait_ge(w_lo_done, j + SLOTS + 1)
                        for t in range(TOKEN_TILES):
                            v_tile(0, t, units, units[0] == 0, False)
                elif k < KT - 1:
                    for t in range(TOKEN_TILES):
                        v_tile(k, t, (0, SLOTS), False, False)
            v_end(KT - 1, range(TOKEN_TILES))
            with pe.Fori(0, DEPTH) as l:
                u0, ea, ed, xs = l * UNITS, l * EA, l * ED, l * XS
                for j in range(2 * SLOTS):
                    if j in (2, 3):
                        pe.wait_ge(v_centered, l * TOKEN_TILES + j)
                    elif j >= SLOTS:
                        pe.wait_ge(evac_act, ea + (EA_QK + j - SLOTS + 1))
                    unit(u0 + (U_QK + j), j % SLOTS, QK_BANK[j % SLOTS], h_hi, h_lo)
                with pe.Fori(0, HEADS) as h:
                    uh = u0 + h * SLOTS + U_HEAD
                    pe.wait_ge(evac_act, ea + h * 2 + (EA_HEAD - 1))
                    unit(uh, 0, 0, h_hi, h_lo)
                    pe.wait_ge(cur_ready, l * HEADS + h + 1)
                    pe.wait_ge(qk_split, l * HEADS + h + 1)
                    pe.wait_ge(std_ready, l * HEADS + h + 1)
                    for jt in range(TOKEN_TILES - 1):
                        out = ps[:, S_BANK[jt], S_COL[jt]:S_COL[jt] + T - jt * P]
                        keys, queries = slice(jt * P, (jt + 1) * P), slice(jt * P, T)
                        for i, (k, q) in enumerate(((k_hi, q_hi), (k_hi, q_lo), (k_lo, q_hi))):
                            mm = nc.tensor.matmul(out, k[:, keys], q[:, queries], start=(i == 0), stop=(i == 2),
                                                  skip_group_check=True)
                        if jt != 2:
                            mm.then_inc(s_ps, 1)
                    nc.tensor.matmul(ps[:, S_BANK[3], S_COL[3]:S_COL[3] + P], k_last[:],
                                     qkT[:, bass.ds(h * 2, 1), 3 * P:T].rearrange("p a t -> p (a t)"),
                                     start=False, stop=True, skip_group_check=True).then_inc(s_ps, 1)
                    pe.wait_ge(evac_act, ea + h * 2 + EA_HEAD)
                    unit(uh + 1, 1, 1, h_hi, h_lo)
                    pe.wait_ge(o_read, l * HEADS + h + 1)
                    for jt in range(TOKEN_TILES):
                        pe.wait_ge(s_ready, l * 16 + h * 4 + (jt + 1))
                        n = T - jt * P
                        mm = nc.tensor.matmul(ps[:, O, jt * P:T], v_cur[:, jt * P:(jt + 1) * P],
                                              s_T[:, S_AT[jt]:S_AT[jt] + n], start=(jt == 0), stop=(jt == 3),
                                              skip_group_check=True)
                    mm.then_inc(o_ps, 1)
                    pe.wait_ge(evac_dve, ed + h * 2 + 1)
                    unit(uh + 2, 2, 2, h_hi, h_lo)
                    pe.wait_ge(osq_split, l * HEADS + h + 1)
                    nc.tensor.matmul(ps[:, STAT, :], mean_e[:], osq_hi[:], start=True, stop=False)
                    nc.tensor.matmul(ps[:, STAT, :], mean_e[:], osq_lo[:], start=False, stop=True).then_inc(var_ps, 1)
                    pe.wait_ge(evac_dve, ed + h * 2 + 2)
                    unit(uh + 3, 3, 3, h_hi, h_lo)
                for k0, k1 in ((0, 6), (6, KT)):
                    for j in range(SLOTS):
                        if k0 == 0:
                            pe.wait_ge(w_lo_done, u0 + (U_OUT + j + SLOTS + 1))
                        for k in range(k0, k1):
                            if j == 0:
                                pe.wait_ge(xs_lo, xs + (XS_Y + k + 1))
                            mm = three(j, j, k, y_hi[:, k, :], y_lo[:, k, :], k == 0, k == KT - 1)
                        if k0:
                            mm.then_inc(pe_unit, 1)
                n, added = l * 2 + 1, l * SQ
                for half in range(2):
                    for j in range(SLOTS):
                        if half == 0:
                            pe.wait_ge(w_lo_done, u0 + (U_OUT + SLOTS + j + SLOTS + 1))
                        if half or j >= 2:
                            pe.wait_ge(evac_dve, ed + (2 + ED_OUT + (j + 3 if half else j - 1)))
                        unit_half(j, OUT_BANK[half][j], half, y_hi, y_lo)
                        if half and j == 0:
                            mean_squares(n, 0, added + (SQ_MIX - SLOTS))
                        if half and j == 1:
                            spread(n, 0, HALVES[0])
                for half in range(2):
                    if half == 0:
                        first_step(u0 + U_UP[0], xs + XS_H2, n, added + SQ_MIX)
                    with pe.Fori(1 - half, 4) as i:
                        for j in range(SLOTS):
                            pe.wait_ge(evac_act, ea + i * 4 + (EA_UP[half] - 4 + j + 1))
                            if half and j >= 2:
                                pe.wait_ge(evac_dve, ed + (2 + ED_DOWN[0] + 5 + j))
                            unit(u0 + i * SLOTS + (U_UP[half] + j), j, j, h_hi, h_lo)
                    with pe.Fori(0, 4 - half) as i:
                        for m in range(2):
                            pe.wait_ge(evac_act, ea + (EA_UP[half] + 15 + m))
                            pe.wait_ge(evac_dve, ed + i * 2 + (ED_DOWN[half] + m + 1))
                            for kk in range(2):
                                pe.wait_ge(xs_lo, xs + (XS_U[half] + 8 * (kk + 1)))
                                unit(u0 + i * SLOTS + (U_DOWN[half] + 2 * m + kk), 2 * m + kk, 2 + m, u_hi, u_lo,
                                     k0=8 * kk, first=(kk == 0), last=(kk == 1))
                n, added = l * 2 + 2, l * SQ + SQ_MIX
                for half in range(2):
                    for m in range(2):
                        if half == 0:
                            pe.wait_ge(evac_dve, ed + (ED_DOWN[1] + 6 + m + 1))
                        for kk in range(2):
                            if half == 0:
                                pe.wait_ge(w_lo_done, u0 + (U_DOWN[1] + 12 + 2 * m + kk + SLOTS + 1))
                            unit_half(2 * m + kk, DOWN_BANK[half][m], half, u_hi, u_lo,
                                      k0=8 * kk, first=(kk == 0), last=(kk == 1))
                            if half and m == 0 and kk == 0:
                                mean_squares(n, 0, added + (SQ_MLP - 2))
                            if half and m == 0 and kk == 1:
                                spread(n, 0, HALVES[0])
                with pe.If(l < DEPTH - 1):
                    v_step(u0 + UNITS, xs + XS, n, added + SQ_MLP)
            mean_squares(2 * DEPTH, 1, DEPTH * SQ)
            pe.wait_ge(out_ready, KT)
            spread(2 * DEPTH, 1, HALVES[1])

        @block.scalar
        def _(act):
            def split_hi(l, step, j):
                u = l * UNITS + step * SLOTS + (SLOTS + j)
                act.wait_ge(w_in[j], (l * STEPS + step) * 16 + 32)
                act.wait_ge(pe_unit, u + 1)
                nc.scalar.copy(w_hi[:, j, :], w_raw[:, j, :]).then_inc(w_hi_done, 1)

            def pe_has(l, u):
                act.wait_ge(pe_unit, l * UNITS + u + (SLOTS + 1))

            def qk_high(l, h):
                act.wait_ge(rope_done, l * 8 + h * 2 + 4)
                nc.scalar.copy(q_hi[:], qkT[:, bass.ds(h * 2, 1), :].rearrange("p a t -> p (a t)"))
                nc.scalar.copy(k_hi[:], qkT[:, bass.ds(h * 2 + 1, 1), :].rearrange("p a t -> p (a t)")
                               ).then_inc(qk_hi_done, 1)

            def norm_root(n, half, tiles=2):
                act.wait_ge(stat_ps, n * 2 + half)
                t = slice(half * 2, half * 2 + 2) if tiles == 2 else slice(0, tiles)
                nc.scalar.activation(std[:, t], ps[:, STAT, t], ACT.Sqrt, bias=eps[:, 0:1]).then_inc(norm_std, 1)

            def high(n, which, half, k):
                shift = 2 * k if which == 0 else M_SH2 + k
                act.wait_ge(xr_ready, n * 16 + (half * KT + k - 7))
                nc.scalar.activation(h_hi[:, k, HALVES[half]], ring[k % 4][:, HALVES[half]], ACT.Identity,
                                     bias=mod[:, shift:shift + 1]).then_inc(xs_hi, 1)

            def square(added, s, xk, at=WHOLE):
                act.wait_ge(ssum_added, added + s + 1)
                nc.scalar.activation(buf_a[:, s % 2, at], xk, ACT.Square).then_inc(sq_ready, 1)

            def between(l, step, n, which, squares):
                def tiles(*ks):
                    for k in ks:
                        high(n, which, 0, k)
                squares(0)
                norm_root(n, 0)
                split_hi(l, step, 0)
                split_hi(l, step, 1)
                tiles(0, 1)
                squares(1)
                tiles(2, 3)
                squares(2)
                tiles(4)
                split_hi(l, step, 2)
                tiles(5, 6)
                squares(3)
                tiles(7)
                split_hi(l, step, 3)
                norm_root(n, 1)
                for k in range(KT):
                    high(n, which, 1, k)

            act.sem_inc(std_ready, 1)
            act.wait_ge(c_in, 32)
            nc.scalar.activation(c_col[:, 1, :], c_col[:, 0, :], ACT.Exp, scale=-1.0).then_inc(c_exp, 1)
            for m in range(KT):
                act.wait_ge(x_in[m // 4], 16)
                if m >= 4:
                    act.wait_ge(x_added, max(m - 4, 1))
                nc.scalar.activation(ring[m % 4], x[:, m, :], ACT.Square).then_inc(x_squared, 1)
                if m in (1, 3):
                    half = HALVES_D[m // 2]
                    act.wait_ge(c_ps, m // 2 + 1)
                    nc.scalar.copy(c_act[:, half], ps[:, m // 2, :]).then_inc(c_ready, 1)
            act.wait_ge(consts, 1)
            nc.scalar.activation(mean_e[:], ones[:], ACT.Copy, scale=1.0 / P).then_inc(mean_ready, 1)
            nc.scalar.activation(warm[:], eps[:], ACT.Sqrt)

            def first_split(j):
                act.wait_ge(w_in[j], 16)
                nc.scalar.copy(w_hi[:, j, :], w_raw[:, j, :]).then_inc(w_hi_done, 1)

            def first_shift(k):
                act.wait_ge(sh_product, k + 1)
                nc.scalar.activation(arena[:, 2 * k, :], arena[:, 2 * k, :], ACT.Identity,
                                     accum_out=sh_sum[:, k:k + 1]).then_inc(sh_summed, 1)
                act.wait_ge(sh_summed, k + 1)
                nc.scalar.activation(mod[:, 2 * k:2 * k + 1], sh_sum[:, k:k + 1], ACT.Identity,
                                     bias=bia[:, 2 * k:2 * k + 1]).then_inc(sh_ready, 1)

            def first_high(k):
                act.wait_ge(xr_ready, k + 1)
                act.wait_ge(sh_ready, k + 1)
                nc.scalar.activation(h_hi[:, k, :], ring[k % 4], ACT.Identity, bias=mod[:, 2 * k:2 * k + 1]
                                     ).then_inc(xs_hi, 2)

            first_split(0)
            norm_root(0, 1, TOKEN_TILES)
            first_split(1)
            act.wait_ge(par_in, 48)
            first_shift(0)
            first_split(2)
            first_high(0)
            first_split(3)
            for k in range(1, KT):
                first_shift(k)
                first_high(k)

            with act.Fori(0, DEPTH) as l:
                for j in range(SLOTS):
                    split_hi(l, 0, j)
                for i in range(2):
                    for j in range(SLOTS):
                        bank = QK_BANK[j]
                        pe_has(l, i * 4 + (U_QK + j))
                        act.wait_ge(rope_done, l * 8 + i * 4 + (j + 1))
                        nc.scalar.copy(buf_b[0:64, j % 2, :], ps[64:128, bank, :])
                        nc.scalar.copy(buf_b[64:128, j % 2, :], ps[0:64, bank, :])
                        nc.scalar.copy(buf_a[:, j % 2, :], ps[:, bank, :]).then_inc(evac_act, 1)
                        split_hi(l, i + 1, j)
                        if i == 1 and j == 1:
                            qk_high(l, 0)
                with act.Fori(0, HEADS) as h:
                    n = l * HEADS + h
                    pe_has(l, h * 4 + U_HEAD)
                    nc.scalar.activation(egr[:], ps[:, 0, :], ACT.Exp, scale=-1.0)
                    nc.scalar.copy(gr[:], ps[:, 0, :]).then_inc(evac_act, 1)
                    split_hi(l, h + 3, 0)
                    pe_has(l, h * 4 + (U_HEAD + 1))
                    nc.scalar.copy(cc, ps[:, 1, :]).then_inc(evac_act, 1)
                    split_hi(l, h + 3, 1)
                    act.wait_ge(rope_done, l * 8 + 10)
                    act.wait_ge(o_ps, n + 2)
                    nc.scalar.activation(buf_a[:, 0, :], ps[:, O, :], ACT.Square).then_inc(osq_ready, 1)
                    act.wait_ge(osq_ready, n + 1)
                    nc.scalar.copy(osq_hi[:], buf_a[:, 0, :]).then_inc(osq_hi_done, 1)
                    split_hi(l, h + 3, 2)
                    act.wait_ge(var_ps, n + 1)
                    nc.scalar.activation(buf_a[:, 1, :], ps[:, STAT, :], ACT.Sqrt, bias=eps[:, 0:1]).then_inc(std_ready, 1)
                    with act.If(h < HEADS - 1):
                        qk_high(l, below(h + 1, HEADS))
                    act.wait_ge(evac_dve, l * ED + h * 2 + (ED_HEAD + 4))
                    nc.scalar.copy(y_hi[:, bass.ds(h * 2, 1), :].rearrange("p a t -> p (a t)"), conv).then_inc(xs_hi, 1)
                    act.wait_ge(gate_step, n * 3 + 3)
                    nc.scalar.copy(y_hi[:, bass.ds(h * 2 + 1, 1), :].rearrange("p a t -> p (a t)"), buf_b[:, 1, :]
                                   ).then_inc(xs_hi, 1)
                    split_hi(l, h + 3, 3)
                added = l * SQ
                for m in range(SLOTS):
                    split_hi(l, 7, m)
                    act.wait_ge(evac_dve, l * ED + (2 + ED_OUT + m + 1))
                    square(added, m, x[:, m, :])

                def out_square(half, j):
                    act.wait_ge(evac_dve, l * ED + (2 + ED_OUT + (half + 1) * SLOTS + j + 1))
                    square(added, (half + 1) * SLOTS + j, x[:, SLOTS + j, HALVES[half]], HALVES[half])

                for j in range(SLOTS):
                    out_square(0, j)
                between(l, 8, l * 2 + 1, 1, lambda j: out_square(1, j))
                for half in range(2):
                    with act.Fori(0, 4) as i:
                        for j in range(SLOTS):
                            pe_has(l, i * 4 + (U_UP[half] + j))
                            nc.scalar.activation(buf_a[:, j % 2, :], ps[:, j, :], ACT.Relu).then_inc(evac_act, 1)
                            split_hi(l, i + (9 + 8 * half), j)
                            act.wait_ge(rsq_ready, l * 32 + i * 4 + (16 * half + j + 1))
                            nc.scalar.copy(u_hi[:, bass.ds(i * 4 + j, 1), :].rearrange("p a t -> p (a t)"),
                                           buf_b[:, j % 2, :]).then_inc(xs_hi, 1)
                    if half == 0:
                        with act.Fori(0, 4) as i:
                            for j in range(SLOTS):
                                split_hi(l, i + 13, j)

                added = l * SQ + SQ_MIX
                with act.Fori(0, 3) as i:
                    for m in range(2):
                        split_hi(l, i + 21, 2 * m)
                        act.wait_ge(evac_dve, l * ED + i * 2 + (2 + ED_DOWN[1] + m + 1))
                        act.wait_ge(ssum_added, added + i * 2 + m + 1)
                        nc.scalar.activation(buf_a[:, m, :], x[:, bass.ds(i * 2 + m, 1), :].rearrange("p a t -> p (a t)"),
                                             ACT.Square).then_inc(sq_ready, 1)
                        split_hi(l, i + 21, 2 * m + 1)

                def down_square(half, m):
                    act.wait_ge(evac_dve, l * ED + (2 + ED_DOWN[1] + 6 + half * 2 + m + 1))
                    square(added, 6 + half * 2 + m, x[:, 6 + m, HALVES[half]], HALVES[half])

                for m in range(2):
                    down_square(0, m)
                with act.If(l < DEPTH - 1):
                    between(l, 24, l * 2 + 2, 0, lambda j: down_square(1, j // 2) if j % 2 else None)
                with act.If(l > DEPTH - 2):
                    norm_root(l * 2 + 2, 0)
                    down_square(1, 0)
                    down_square(1, 1)
                    norm_root(l * 2 + 2, 1)

        @block.vector
        def _(dve):
            def split_lo(l, step, j):
                dve.wait_ge(w_hi_done, l * UNITS + step * SLOTS + (SLOTS + j + 1))
                nc.vector.tensor_tensor(w_lo[:, j, :], w_raw[:, j, :], w_hi[:, j, :].bitcast(F32), ALU.subtract
                                        ).then_inc(w_lo_done, 1)

            def pe_has(l, u):
                dve.wait_ge(pe_unit, l * UNITS + u + (SLOTS + 1))

            def reduce_ada(use, slot, j, pair):
                dve.wait_ge(ada_in[slot], use * 16 + 16)
                if j == 0:
                    dve.wait_ge(mod_added, pair + KT)
                nc.vector.tensor_tensor_reduce(out=ada_raw[:, slot, :], in0=ada_raw[:, slot, :], in1=c_act[:],
                                               scale=1.0, scalar=0.0, op0=ALU.mult, op1=ALU.add,
                                               accum_out=ada_sum[:, j:j + 1]).then_inc(ada_done, 1)

            def add_bias(pair, col):
                dve.wait_ge(ada_done, pair * 2 + (SLOTS + 2))
                nc.vector.tensor_tensor(mod[:, bass.ds(col, 2)], ada_sum[:],
                                        bia[:, bass.ds(below(pair * 2 + FIRST_MODS, DEPTH * MODS, 2), 2)],
                                        ALU.add).then_inc(mod_added, 1)

            def early_ada(l, b):
                pair = l * (MODS // 2) + b // 2
                reduce_ada(l * (4 if b % SLOTS >= 2 else 20) + b // SLOTS, b % SLOTS, b % 2, pair)
                if b % 2:
                    add_bias(pair, FIRST_MODS + b - 1)

            def ada_pair(l, p, col, j, later=False):
                if isinstance(p, int) and p == 11:
                    reduce_ada(l * 4 + 3, 2 + j, j, l * (MODS // 2) + p)
                else:
                    reduce_ada(l * 20 + p - (4 if later else 3), j, j, l * (MODS // 2) + p)
                if j:
                    add_bias(l * (MODS // 2) + p, col)

            def xs_low(l, i, out, full, hi):
                dve.wait_ge(xs_hi, l * XS + i + 1)
                nc.vector.tensor_tensor(out, full, hi.bitcast(F32), ALU.subtract).then_inc(xs_lo, 1)

            def norm_scale(n, half, tiles=2):
                t0 = half * 2 if tiles == 2 else 0
                dve.wait_ge(norm_std, n * 2 + half)
                nc.vector.reciprocal(rstd[:, t0:t0 + tiles], std[:, t0:t0 + tiles]).then_inc(norm_r, 1)
                dve.wait_ge(norm_r, n * 4 + (half * 2 - 1))
                nc.vector.tensor_tensor(ssum[:, t0 * P:(t0 + tiles) * P].rearrange("p (a b) -> p a b", b=P),
                                        ident[:].unsqueeze(1).to_broadcast([P, tiles, P]),
                                        rstd[:, t0:t0 + tiles].unsqueeze(2).to_broadcast([P, tiles, P]), ALU.mult
                                        ).then_inc(norm_r, 1)

            def norm_gain(n, which, scale, g):
                nc.vector.scalar_tensor_tensor(out=gm[:, which, :], in0=scale, scalar=1.0, in1=g,
                                               op0=ALU.add, op1=ALU.mult).then_inc(gm_ready, 1)

            def product(xs, n, which, half, k):
                if k == 0:
                    dve.wait_ge(gm_ready, n + (KT - 1) + 1)
                    dve.wait_ge(rinv_ps, n * 2 + half)
                if k >= 4:
                    dve.wait_ge(xs_lo, xs + (half * KT + k - 3))
                at = HALVES[half]
                nc.vector.scalar_tensor_tensor(out=ring[k % 4][:, at], in0=x[:, k, at], scalar=gm[:, which, k:k + 1],
                                               in1=rinv[:, at], op0=ALU.mult, op1=ALU.mult).then_inc(xr_ready, 1)

            def low(xs, which, half, k):
                shift = 2 * k if which == 0 else M_SH2 + k
                at = HALVES[half]
                dve.wait_ge(xs_hi, xs + (half * KT + k + 1))
                nc.vector.scalar_tensor_tensor(out=h_lo[:, k, at], in0=ring[k % 4][:, at],
                                               scalar=mod[:, shift:shift + 1], in1=h_hi[:, k, at].bitcast(F32),
                                               op0=ALU.add, op1=ALU.subtract).then_inc(xs_lo, 1)

            def between(l, step, xs, n, which, rest):
                def tiles(half, *ks):
                    for k in ks:
                        if k < KT:
                            product(xs, n, which, half, k)
                        if k:
                            low(xs, which, half, k - 1)
                rest(0)
                norm_scale(n, 0)
                split_lo(l, step, 0)
                tiles(0, 0, 1)
                rest(1)
                tiles(0, 2, 3, 4)
                rest(2)
                tiles(0, 5, 6)
                rest(3)
                tiles(0, 7, 8)
                dve.wait_ge(w_lo_done, l * UNITS + (step * SLOTS + 2 * SLOTS + 2))
                split_lo(l, step, 2)
                split_lo(l, step, 3)
                norm_scale(n, 1)
                tiles(1, *range(KT + 1))

            def final(half):
                at = HALVES[half]
                dve.wait_ge(rinv_ps, 4 * DEPTH + half)
                for k in range(KT):
                    nc.vector.scalar_tensor_tensor(out=x[:, k, at], in0=x[:, k, at], scalar=fin_g[:, k:k + 1],
                                                   in1=rinv[:, at], op0=ALU.mult, op1=ALU.mult).then_inc(out_ready, 1)

            def qk_low(l, h):
                dve.wait_ge(qk_hi_done, l * HEADS + h + 1)
                nc.vector.tensor_tensor(q_lo[:], qkT[:, bass.ds(h * 2, 1), :].rearrange("p a t -> p (a t)"),
                                        q_hi[:].bitcast(F32), ALU.subtract)
                nc.vector.tensor_tensor(k_lo[:], qkT[:, bass.ds(h * 2 + 1, 1), :].rearrange("p a t -> p (a t)"),
                                        k_hi[:].bitcast(F32), ALU.subtract).then_inc(qk_split, 1)

            def center_v(l, i, t):
                if t < 3:
                    dve.wait_ge(v_ready, l * 3 + (t + 1))
                else:
                    pe_has(l, U_V + 3)
                dve.wait_ge(v_centered, l * TOKEN_TILES + (i + 1))
                vp = ps[:, t, :].rearrange("p (h e) -> p h e", e=P)
                nc.vector.tensor_reduce(vsum[:], vp, AX_X, ALU.add).then_inc(v_summed, 1)
                dve.wait_ge(v_summed, l * TOKEN_TILES + (i + 1))
                nc.vector.scalar_tensor_tensor(
                    out=v_tok[:, :, t * P:(t + 1) * P], in0=vsum[:].unsqueeze(2).to_broadcast([P, HEADS, P]),
                    scalar=-1.0 / P, in1=vp, op0=ALU.mult, op1=ALU.add).then_inc(v_centered, 1)

            def residual(m, bank, gate_col, at=WHOLE):
                xm = x[:, bass.ds(m, 1), at].rearrange("p a t -> p (a t)")
                nc.vector.scalar_tensor_tensor(out=xm, in0=ps[:, bank, at], scalar=mod[:, bass.ds(m + gate_col, 1)],
                                               in1=xm, op0=ALU.mult, op1=ALU.add).then_inc(evac_dve, 1)

            dve.sem_inc(w_lo_done, SLOTS)
            dve.sem_inc(ada_done, SLOTS)
            dve.sem_inc(evac_dve, 2)
            dve.sem_inc(mod_added, KT)
            for s in (v_centered, o_read, conv_step):
                dve.sem_inc(s, 1)
            nc.vector.memset(eps[:], EPS)
            nc.vector.memset(z[:], 0.0)
            nc.vector.memset(mean_d[:], 1.0 / D)
            nc.vector.memset(ones[:], 1.0).then_inc(consts, 1)
            dve.wait_ge(c_exp, 1)
            nc.vector.tensor_scalar(c_col[:, 1, :], c_col[:, 1, :], 1.0, None, ALU.add).then_inc(c_step, 1)
            dve.wait_ge(c_step, 1)
            nc.vector.reciprocal(c_col[:, 1, :], c_col[:, 1, :]).then_inc(c_step, 1)
            dve.wait_ge(c_step, 2)
            nc.vector.tensor_tensor(c_col[:, 1, :], c_col[:, 0, :], c_col[:, 1, :], ALU.mult).then_inc(c_step, 1)
            dve.wait_ge(c_step, 3)
            for i in range(2):
                at = slice(i * TOKEN_TILES, (i + 1) * TOKEN_TILES)
                nc.vector.tensor_tensor(ada_raw[:, 0, HALVES_D[i]].rearrange("p (a b) -> p a b", b=P),
                                        ident[:].unsqueeze(1).to_broadcast([P, KT // 2, P]),
                                        c_col[:, 1, at].unsqueeze(2).to_broadcast([P, KT // 2, P]), ALU.mult
                                        ).then_inc(c_step, 1)
            for m in range(1, KT):
                dve.wait_ge(x_squared, m + 1)
                if m > 1:
                    dve.wait_ge(x_added, m - 1)
                nc.vector.tensor_tensor(ssum[:], ring[0] if m == 1 else ssum[:], ring[m % 4], ALU.add
                                        ).then_inc(x_added, 1)
            dve.wait_ge(par_in, 48)
            nc.vector.tensor_scalar(sc_bias[:], bia[:, 1:2 * KT:2], 1.0, None, ALU.add).then_inc(sc_summed, 1)
            dve.wait_ge(c_ready, 2)

            def first_scale(k):
                dve.wait_ge(sc_in[k], 16)
                nc.vector.tensor_tensor_reduce(out=arena[:, 2 * k + 1, :], in0=arena[:, 2 * k + 1, :], in1=c_act[:],
                                               scale=1.0, scalar=0.0, op0=ALU.mult, op1=ALU.add,
                                               accum_out=sc_sum[:, k:k + 1]).then_inc(sc_summed, 1)

            def first_gain(k):
                dve.wait_ge(sc_summed, k + 2)
                nc.vector.scalar_tensor_tensor(out=gm[:, 0, k:k + 1], in0=sc_sum[:, k:k + 1], scalar=sc_bias[:, k:k + 1],
                                               in1=par[:, C_G1 + k:C_G1 + k + 1], op0=ALU.add, op1=ALU.mult
                                               ).then_inc(gm_ready, 1)

            def first_product(k):
                if k == 0:
                    dve.wait_ge(rinv_ps, 1)
                if k >= 4:
                    dve.wait_ge(xs_lo, 2 * k - 6)
                dve.wait_ge(gm_ready, k + 1)
                nc.vector.scalar_tensor_tensor(out=ring[k % 4], in0=x[:, k, :], scalar=gm[:, 0, k:k + 1],
                                               in1=rinv, op0=ALU.mult, op1=ALU.mult).then_inc(xr_ready, 1)

            def first_low(k):
                dve.wait_ge(xs_hi, 2 * k + 2)
                nc.vector.scalar_tensor_tensor(out=h_lo[:, k, :], in0=ring[k % 4], scalar=mod[:, 2 * k:2 * k + 1],
                                               in1=h_hi[:, k, :].bitcast(F32), op0=ALU.add, op1=ALU.subtract
                                               ).then_inc(xs_lo, 2)

            first_scale(0)
            for j in range(SLOTS):
                if j == 1:
                    norm_scale(0, 1, TOKEN_TILES)
                if j == 2:
                    first_gain(0)
                    first_product(0)
                dve.wait_ge(w_hi_done, j + 1)
                nc.vector.tensor_tensor(w_lo[:, j, :], w_raw[:, j, :], w_hi[:, j, :].bitcast(F32), ALU.subtract
                                        ).then_inc(w_lo_done, 1)
                if j == 2:
                    first_low(0)
            for k in range(1, KT):
                first_scale(k)
                first_gain(k)
                if k > 1:
                    first_low(k - 1)
                first_product(k)
            first_low(KT - 1)

            with dve.Fori(0, DEPTH) as l:
                split_lo(l, 0, 0)
                split_lo(l, 0, 1)
                for i in range(2):
                    center_v(l, i, 2 + i)
                    split_lo(l, 0, 2 + i)
                center_v(l, 2, 0)
                center_v(l, 3, 1)
                for j in range(SLOTS):
                    early_ada(l, j)
                for j in range(SLOTS):
                    split_lo(l, 1, j)
                    early_ada(l, 4 + j)
                for j in range(SLOTS):
                    split_lo(l, 2, j)
                    if j == 2:
                        qk_low(l, 0)
                    early_ada(l, 8 + j)
                dve.wait_ge(decay_in, 16)
                with dve.Fori(0, HEADS) as h:
                    n = l * HEADS + h
                    for jt in range(TOKEN_TILES):
                        if jt != 3:
                            dve.wait_ge(s_ps, n * 3 + (jt + 1))
                        w = T - jt * P
                        nc.vector.tensor_tensor(s_T[:, S_AT[jt]:S_AT[jt] + w],
                                                ps[:, S_BANK[jt], S_COL[jt]:S_COL[jt] + w],
                                                decay[:, bass.ds(h, 1), 0:w].rearrange("p a t -> p (a t)"), ALU.mult
                                                ).then_inc(s_ready, 1)
                    split_lo(l, h + 3, 0)
                    ada_pair(l, h + 6, h * 2 + (FIRST_MODS + 12), 0)
                    split_lo(l, h + 3, 1)
                    ada_pair(l, h + 6, h * 2 + (FIRST_MODS + 12), 1)
                    dve.wait_ge(osq_hi_done, n + 1)
                    nc.vector.tensor_tensor(osq_lo[:], buf_a[:, 0, :], osq_hi[:].bitcast(F32), ALU.subtract
                                            ).then_inc(osq_split, 1)
                    pe_has(l, h * 4 + (U_HEAD + 2))
                    dve.wait_ge(evac_act, l * EA + h * 2 + (EA_HEAD + 2))
                    dve.wait_ge(conv_step, n * 3 + 1)
                    nc.vector.tensor_tensor(z[:, 2:T + 2], ps[:, 2, :], cc, ALU.mult).then_inc(evac_dve, 1)
                    split_lo(l, h + 3, 2)
                    tap = [par[:, bass.ds(l * PARAMS + h * 3 + (C_CONV + t), 1)] for t in range(3)]
                    dve.wait_ge(evac_dve, l * ED + h * 2 + (2 + ED_HEAD + 1))
                    dve.wait_ge(xs_lo, l * XS + h * 2 + XS_Y)
                    nc.vector.tensor_scalar(conv, z[:, 0:T], tap[0], None, ALU.mult).then_inc(conv_step, 1)
                    for t in (1, 2):
                        dve.wait_ge(conv_step, n * 3 + (t + 1))
                        nc.vector.scalar_tensor_tensor(out=conv, in0=z[:, t:t + T], scalar=tap[t], in1=conv,
                                                       op0=ALU.mult, op1=ALU.add).then_inc(conv_step, 1)
                    dve.wait_ge(var_ps, n + 1)
                    nc.vector.scalar_tensor_tensor(out=buf_b[:, 1, :], in0=ps[:, O, :],
                                                   scalar=par[:, bass.ds(l * PARAMS + h + C_RET, 1)], in1=gr[:],
                                                   op0=ALU.mult, op1=ALU.mult).then_inc(o_read, 1)
                    dve.wait_ge(std_ready, n + 2)
                    nc.vector.scalar_tensor_tensor(out=egr[:], in0=egr[:], scalar=1.0, in1=buf_a[:, 1, :],
                                                   op0=ALU.add, op1=ALU.mult).then_inc(gate_step, 1)
                    with dve.If(h < HEADS - 1):
                        qk_low(l, below(h + 1, HEADS))
                    dve.wait_ge(gate_step, n * 3 + 1)
                    nc.vector.reciprocal(buf_b[:, 0, :], egr[:]).then_inc(gate_step, 1)
                    pe_has(l, h * 4 + (U_HEAD + 3))
                    dve.wait_ge(conv_step, n * 3 + 4)
                    nc.vector.tensor_tensor(conv, ps[:, 3, :], conv, ALU.mult).then_inc(evac_dve, 1)
                    dve.wait_ge(gate_step, n * 3 + 2)
                    nc.vector.tensor_tensor(buf_b[:, 1, :], buf_b[:, 1, :], buf_b[:, 0, :], ALU.mult
                                            ).then_inc(gate_step, 1)
                    xs_low(l, h * 2 + XS_Y, y_lo[:, bass.ds(h * 2, 1), :].rearrange("p a t -> p (a t)"), conv,
                           y_hi[:, bass.ds(h * 2, 1), :].rearrange("p a t -> p (a t)"))
                    xs_low(l, h * 2 + (XS_Y + 1), y_lo[:, bass.ds(h * 2 + 1, 1), :].rearrange("p a t -> p (a t)"),
                           buf_b[:, 1, :], y_hi[:, bass.ds(h * 2 + 1, 1), :].rearrange("p a t -> p (a t)"))
                    split_lo(l, h + 3, 3)
                for j in range(SLOTS):
                    ada_pair(l, 10 + j // 2, FIRST_MODS + 20 + j // 2 * 2, j % 2)
                dve.wait_ge(mod_added, l * 24 + 12)
                for j in range(SLOTS):
                    pe_has(l, U_OUT + j)
                    residual(j, j, M_GATE1)
                    split_lo(l, 7, j)

                def out_rest(j):
                    pe_has(l, U_OUT + SLOTS + j)
                    residual(SLOTS + j, OUT_BANK[1][j], M_GATE1, HALVES[1])

                for j in range(SLOTS):
                    dve.wait_ge(pe_half, l * 6 + j + 1)
                    residual(SLOTS + j, OUT_BANK[0][j], M_GATE1, HALVES[0])
                dve.wait_ge(mod_added, l * 24 + 20)
                norm_gain(l * 2 + 1, 1, mod[:, M_SC2:M_SC2 + KT], par[:, bass.ds(l * PARAMS + C_G2, KT)])
                between(l, 8, l * XS + XS_H2, l * 2 + 1, 1, out_rest)
                for half in range(2):
                    with dve.Fori(0, 4) as i:
                        for j in range(SLOTS):
                            split_lo(l, i + (9 + 8 * half), j)
                            ub = bass.ds(i * 4 + j, 1)
                            xs_low(l, i * 4 + (XS_U[half] + j), u_lo[:, ub, :].rearrange("p a t -> p (a t)"),
                                   buf_b[:, j % 2, :], u_hi[:, ub, :].rearrange("p a t -> p (a t)"))
                            if half == 0 and j < 2:
                                ada_pair(l, i + 12, i * 2 + M_GATE2, j, later=True)
                        if half:
                            with dve.If(l < DEPTH - 1):
                                for j in range(2):
                                    ada_pair(l, i + 20, i * 2 + KT, j, later=True)
                    if half == 0:
                        with dve.Fori(0, 4) as i:
                            for m in range(2):
                                split_lo(l, i + 13, 2 * m)
                                pe_has(l, i * 4 + (U_DOWN[0] + 2 * m + 1))
                                dve.wait_ge(mod_added, l * 24 + 24)
                                residual(i * 2 + m, 2 + m, M_GATE2)
                                split_lo(l, i + 13, 2 * m + 1)
                            with dve.If(l < DEPTH - 1):
                                for j in range(2):
                                    ada_pair(l, i + 16, i * 2, j, later=True)
                    else:
                        with dve.Fori(0, 3) as i:
                            for m in range(2):
                                split_lo(l, i + 21, 2 * m)
                                pe_has(l, i * 4 + (U_DOWN[1] + 2 * m + 1))
                                residual(i * 2 + m, 2 + m, M_GATE2)
                                split_lo(l, i + 21, 2 * m + 1)
                        with dve.If(l < DEPTH - 1):
                            dve.wait_ge(mod_added, l * 24 + 32)
                            norm_gain(l * 2 + 2, 0, mod[:, 1:2 * KT:2],
                                      par[:, bass.ds(below(l * PARAMS + PARAMS + C_G1, DEPTH * PARAMS, KT), KT)])

                        def down_rest(j):
                            if j % 2:
                                m = j // 2
                                pe_has(l, U_DOWN[1] + 13 + 2 * m)
                                residual(6 + m, DOWN_BANK[1][m], M_GATE2, HALVES[1])

                        for m in range(2):
                            dve.wait_ge(pe_half, l * 6 + (SLOTS + m + 1))
                            residual(6 + m, DOWN_BANK[0][m], M_GATE2, HALVES[0])
                        with dve.If(l < DEPTH - 1):
                            between(l, 24, l * XS + XS, l * 2 + 2, 0, down_rest)
                        with dve.If(l > DEPTH - 2):
                            norm_scale(l * 2 + 2, 0)
                            down_rest(1)
                            final(0)
                            down_rest(3)
                            norm_scale(l * 2 + 2, 1)
                            final(1)

        @block.gpsimd
        def _(pool):
            def clear_sum(n):
                pool.wait_ge(rinv_ps, n * 2 - 1)
                zero = z[:, 0:1].to_broadcast([P, T])
                nc.gpsimd.tensor_tensor(ssum[:], zero, zero, ALU.add).then_inc(ssum_clear, 1)

            def add_square(n, added, s, slot, at=WHOLE):
                pool.wait_ge(sq_ready, added + s + 1)
                pool.wait_ge(ssum_clear, n)
                pool.wait_ge(ssum_added, added + s + 2)
                nc.gpsimd.tensor_tensor(ssum[:, at], ssum[:, at], buf_a[:, slot, at], ALU.add).then_inc(ssum_added, 1)

            def split_lo(l, step, j):
                pool.wait_ge(w_hi_done, l * UNITS + step * SLOTS + (SLOTS + j + 1))
                nc.gpsimd.tensor_tensor(w_lo[:, j, :], w_raw[:, j, :], w_hi[:, j, :].bitcast(F32), ALU.subtract
                                        ).then_inc(w_lo_done, 1)

            pool.sem_inc(ssum_added, 2)
            pool.sem_inc(rope_done, 2)
            pool.wait_ge(c_ready, 2)
            for k in range(KT):
                pool.wait_ge(sh_in[k], 16)
                nc.gpsimd.tensor_tensor(arena[:, 2 * k, :], arena[:, 2 * k, :], c_act[:], ALU.mult
                                        ).then_inc(sh_product, 1)
            pool.wait_ge(rope_in, 16)
            with pool.Fori(0, DEPTH) as l:
                def current(h, n, roped):
                    zero = z[:, 0:1].to_broadcast([P, T])
                    pool.wait_ge(rope_done, l * 8 + roped)
                    pool.wait_ge(o_ps, n + 1)
                    nc.gpsimd.tensor_tensor(k_last[:], qkT[:, bass.ds(h * 2 + 1, 1), 3 * P:T].rearrange("p a t -> p (a t)"),
                                            z[:, 0:1].to_broadcast([P, P]), ALU.add)
                    pool.wait_ge(v_centered, n + 2)
                    nc.gpsimd.tensor_tensor(v_cur[:], v_tok[:, bass.ds(h, 1), :].rearrange("p a t -> p (a t)"),
                                            zero, ALU.add).then_inc(cur_ready, 1)

                for j in range(2 * SLOTS):
                    a, b = buf_a[:, j % 2, :], buf_b[:, j % 2, :]
                    pool.wait_ge(evac_act, l * EA + (EA_QK + j + 1))
                    nc.gpsimd.tensor_tensor(a, a, cos, ALU.mult)
                    nc.gpsimd.tensor_tensor(b, b, sin, ALU.mult).then_inc(rope_step, 1)
                    pool.wait_ge(rope_step, l * 8 + (j + 1))
                    nc.gpsimd.tensor_tensor(qkT[:, j, :], a, b, ALU.add).then_inc(rope_done, 1)
                    if j == 5:
                        current(0, l * HEADS, 4)
                with pool.Fori(1, HEADS) as h:
                    current(h, l * HEADS + h, 10)
                clear_sum(l * 2 + 1)
                for s in range(SQ_MIX):
                    if s == 8:
                        pool.wait_ge(w_lo_done, l * UNITS + (8 * SLOTS + 2 * SLOTS + 1))
                        split_lo(l, 8, 1)
                    add_square(l * 2 + 1, l * SQ, s, s % 2, WHOLE if s < SLOTS else HALVES[s // SLOTS - 1])
                for half in range(2):
                    with pool.Fori(0, 4) as i:
                        for j in range(SLOTS):
                            pool.wait_ge(evac_act, l * EA + i * 4 + (EA_UP[half] + j + 1))
                            pool.wait_ge(xs_lo, l * XS + i * 4 + (XS_U[half] + j - 1))
                            nc.gpsimd.tensor_tensor(buf_b[:, j % 2, :], buf_a[:, j % 2, :], buf_a[:, j % 2, :], ALU.mult
                                                    ).then_inc(rsq_ready, 1)
                clear_sum(l * 2 + 2)
                added = l * SQ + SQ_MIX
                with pool.Fori(0, 3) as i:
                    for m in range(2):
                        add_square(l * 2 + 2, added, i * 2 + m, m)
                for s in range(6, SQ_MLP):
                    if s == 8:
                        with pool.If(l < DEPTH - 1):
                            pool.wait_ge(w_lo_done, l * UNITS + (24 * SLOTS + 2 * SLOTS + 1))
                            split_lo(l, 24, 1)
                    add_square(l * 2 + 2, added, s, s % 2, HALVES[(s - 6) // 2])


def shape_tables():
    import numpy as np
    decay = np.zeros((HEADS, P, T), np.float64)
    off = np.arange(T)[None, :] - np.arange(P)[:, None]
    for h in range(HEADS):
        log_g = np.log1p(-np.exp2(-5.0 - h))
        decay[h] = np.where(off >= 0, np.exp(log_g * np.maximum(off, 0)), 0.0) * P ** -0.5
    half = P // 2
    inv = np.float32(10000.0) ** (-np.arange(0, P, 2, dtype=np.float32) / np.float32(P))
    ang = inv[:, None] * np.arange(T, dtype=np.float32)[None, :]
    cos = np.concatenate([np.cos(ang), np.cos(ang)])
    sin = np.concatenate([-np.sin(ang), np.sin(ang)])
    assert cos.shape == (2 * half, T)
    parts = [decay.transpose(1, 0, 2).reshape(P, HEADS * T), cos, sin]
    return np.ascontiguousarray(np.concatenate([p.astype(np.float32) for p in parts], axis=1))


def columns(w):
    k, n = w.shape
    return w.reshape(k // P, P, n // P, P).transpose(2, 0, 1, 3)


def weight_stream(w_in, w_out, w_up, w_down):
    import numpy as np
    units = []
    for l in range(DEPTH):
        t = columns(w_in[l])
        cb, ccs, cu, q, k, v, g = (t[4 * i:4 * i + 4] for i in range(7))
        units += list(v)
        for h in range(HEADS):
            units += [q[h], k[h]]
        for h in range(HEADS):
            units += [g[h], ccs[h], cu[h], cb[h]]
        order = [half * HEADS + h for h in range(HEADS) for half in range(2)]
        units += list(columns(w_out[l])[:, order])
        up, down = columns(w_up[l]), columns(w_down[l])
        for half in range(2):
            units += list(up[half * HALF_TILES:(half + 1) * HALF_TILES])
            for m in range(KT):
                for kk in range(2):
                    k0 = half * HALF_TILES + 8 * kk
                    units.append(down[m, k0:k0 + 8])
    out = np.empty((len(units), P, KT, P), np.float32)
    for i, u in enumerate(units):
        out[i] = u.transpose(1, 0, 2)
    return out.reshape(len(units), P, D)


def kernel(x, c, norm1_g, w_in, conv_w, ret_norm_g, w_out, norm2_g, w_up, w_down, w_ada, b_ada, final_g):
    import numpy as np
    import concourse.bacc as bacc
    from concourse.bass_utils import run_bass_kernel_spmd

    cols = lambda a: np.asarray(a).reshape(-1, P).T
    params = []
    for l in range(DEPTH):
        params += [cols(norm1_g[l]), cols(norm2_g[l]),
                   np.asarray(conv_w[l]).reshape(3, HEADS, P).transpose(2, 1, 0).reshape(P, 12), cols(ret_norm_g[l])]
    mods = [half * KT + k for k in range(KT) for half in range(2)] + list(range(2 * KT, MODS))
    mods = [l * MODS + m for l in range(DEPTH) for m in mods]
    arrays = {
        "xT": np.asarray(x)[0].T.reshape(KT, P, T),
        "c_cols": cols(c),
        "weights": weight_stream(*(np.asarray(w) for w in (w_in, w_out, w_up, w_down))),
        "ada": np.asarray(w_ada).transpose(0, 2, 1).reshape(DEPTH * MODS, P, D)[mods],
        "params": np.concatenate(params, axis=1),
        "bias": cols(b_ada)[:, mods],
        "final_g": cols(final_g),
        "identity": np.eye(P, dtype=np.float32),
        "tables": shape_tables(),
    }
    arrays = {k: np.ascontiguousarray(v) for k, v in arrays.items()}
    nc = bacc.Bacc("TRN2", target_bir_lowering=False, num_devices=1)
    aps = {k: nc.dram_tensor(k, v.shape, mybir.dt.from_np(v.dtype), kind="ExternalInput").ap()
           for k, v in arrays.items()}
    outT = nc.dram_tensor("outT", (KT, P, T), F32, kind="ExternalOutput").ap()
    trunk(nc, **aps, outT=outT)
    result = run_bass_kernel_spmd(nc, [arrays], core_ids=[0])
    return np.ascontiguousarray(result.results[0]["outT"].reshape(D, T).T).reshape(1, T, D)
```
